# Optimizing a Trainium2 kernel written in Bass

```python
import math
import jax, jax.numpy as jnp
from jax import lax
import numpy as np

D_MODEL = 2048
BATCH = 1
SEQ = 256
DEPTH = 1

CHUNK = 64
N_BRANCH = 4
BRANCH_WIDTH = D_MODEL // 2
POOL_WIDTH = BRANCH_WIDTH
POOL_WINDOWS = (2, 4, 8, 16)
POOL_GROUP = POOL_WIDTH // len(POOL_WINDOWS)
SSD_INNER = BRANCH_WIDTH
SSD_HEADDIM = 64
SSD_HEADS = SSD_INNER // SSD_HEADDIM
SSD_STATE = 128
SSD_GROUPS = 4
SSD_HPG = SSD_HEADS // SSD_GROUPS
SSD_CONV = 4
SSD_CONV_DIM = SSD_INNER + 2 * SSD_GROUPS * SSD_STATE
SSD_NORM_GROUPS = SSD_GROUPS
HGRN_KDIM = 128
HGRN_HEADS = BRANCH_WIDTH // HGRN_KDIM
HGRN_VDIM = BRANCH_WIDTH // HGRN_HEADS
HGRN_KEY_WIDTH = HGRN_HEADS * HGRN_KDIM
HGRN_VAL_WIDTH = HGRN_HEADS * HGRN_VDIM
MEM_TOKENS = 256
MEM_HEADS = 4
MEM_WIDTH = BRANCH_WIDTH
MEM_HEAD_DIM = MEM_WIDTH // MEM_HEADS
IN_SPLITS = (POOL_WIDTH, SSD_INNER, SSD_CONV_DIM, SSD_HEADS,
             HGRN_KEY_WIDTH, HGRN_KEY_WIDTH, HGRN_VAL_WIDTH, HGRN_VAL_WIDTH,
             MEM_WIDTH, N_BRANCH * D_MODEL)
IN_COLS = sum(IN_SPLITS)
N_EXPERTS = 64
TOP_K = 8
N_GROUPS = 8
TOPK_GROUPS = 4
D_EXPERT = 256
D_SHARED = 256
ROUTED_SCALE = 2.5
EXPERT_BLOCK = 128
MASK_SCORE = -1e4
ALPHA = (2 * DEPTH) ** 0.25
BETA = (8 * DEPTH) ** -0.25
EPS = 1e-5

kernel_name = "hybrid_pool_ssd_hgrn2_mem_moe_deepnorm"

f32 = jnp.float32

def layer_norm(x, g, b):
    xf = x.astype(f32)
    mu = jnp.mean(xf, -1, keepdims=True)
    var = jnp.mean(jnp.square(xf - mu), -1, keepdims=True)
    return ((xf - mu) * lax.rsqrt(var + EPS) * g.astype(f32) + b.astype(f32)).astype(x.dtype)

def rms_norm(x, w):
    xf = x.astype(f32)
    return xf * lax.rsqrt(jnp.mean(jnp.square(xf), -1, keepdims=True) + EPS) * w.astype(f32)

def pool_mixer(u, pool_w, pool_scale):
    bsz, L, _ = u.shape
    uf = u.astype(f32)
    cs = jnp.concatenate([jnp.zeros((bsz, 1, POOL_WIDTH), f32), jnp.cumsum(uf, axis=1)], axis=1)
    t = jnp.arange(L)
    outs = []
    for gi, w in enumerate(POOL_WINDOWS):
        sl = slice(gi * POOL_GROUP, (gi + 1) * POOL_GROUP)
        lo = jnp.maximum(t + 1 - w, 0)
        win_sum = cs[:, 1:, sl] - cs[:, lo, sl]
        cnt = jnp.minimum(t + 1, w).astype(f32)
        d = win_sum / cnt[None, :, None] - uf[:, :, sl]
        outs.append(d @ pool_w[gi].astype(f32))
    y = jnp.concatenate(outs, axis=-1) * pool_scale.astype(f32)
    return y.astype(u.dtype)

def causal_depthwise_conv(u, w, b):
    k = w.shape[0]
    y = lax.conv_general_dilated(u, w[:, None, :].astype(u.dtype), window_strides=(1,),
                                 padding=[(k - 1, 0)], dimension_numbers=("NWC", "WIO", "NWC"),
                                 feature_group_count=u.shape[-1])
    return y + b.astype(u.dtype)

def decay_matrix(a):
    T = a.shape[-1]
    cs = jnp.cumsum(a, axis=-1)
    diff = cs[..., :, None] - cs[..., None, :]
    mask = jnp.tril(jnp.ones((T, T), bool))
    return jnp.where(mask, jnp.exp(jnp.where(mask, diff, 0.0)), 0.0)

def ssd_mixer(z, xbc, dt_raw, conv_w, conv_b, dt_bias, a_log, d_skip, norm_w):
    bsz, L, _ = z.shape
    nc = L // CHUNK
    xbc = jax.nn.silu(causal_depthwise_conv(xbc, conv_w, conv_b)).astype(f32)
    xs = xbc[..., :SSD_INNER].reshape(bsz, L, SSD_HEADS, SSD_HEADDIM)
    bm = xbc[..., SSD_INNER:SSD_INNER + SSD_GROUPS * SSD_STATE].reshape(bsz, L, SSD_GROUPS, SSD_STATE)
    cm = xbc[..., SSD_INNER + SSD_GROUPS * SSD_STATE:].reshape(bsz, L, SSD_GROUPS, SSD_STATE)
    bm = jnp.repeat(bm, SSD_HPG, axis=2)
    cm = jnp.repeat(cm, SSD_HPG, axis=2)
    dt = jax.nn.softplus(dt_raw.astype(f32) + dt_bias.astype(f32))
    a = -jnp.exp(a_log.astype(f32))
    X = (xs * dt[..., None]).reshape(bsz, nc, CHUNK, SSD_HEADS, SSD_HEADDIM)
    Bc = bm.reshape(bsz, nc, CHUNK, SSD_HEADS, SSD_STATE)
    Cc = cm.reshape(bsz, nc, CHUNK, SSD_HEADS, SSD_STATE)
    Ad = (dt * a).reshape(bsz, nc, CHUNK, SSD_HEADS).transpose(0, 3, 1, 2)
    A_cs = jnp.cumsum(Ad, axis=-1)
    scores = jnp.einsum('bclhn,bcshn->bhcls', Cc, Bc) * decay_matrix(Ad)
    y_diag = jnp.einsum('bhcls,bcshp->bclhp', scores, X)
    decay_states = jnp.exp(A_cs[..., -1:] - A_cs).transpose(0, 2, 3, 1)
    states = jnp.einsum('bclhn,bclhp->bchpn', Bc * decay_states[..., None], X)
    states = jnp.concatenate([jnp.zeros_like(states[:, :1]), states], axis=1)
    chunk_decay = decay_matrix(jnp.pad(A_cs[..., -1], ((0, 0), (0, 0), (1, 0))))
    prev_states = jnp.einsum('bhzc,bchpn->bzhpn', chunk_decay, states)[:, :-1]
    y_off = jnp.einsum('bclhn,bchpn->bclhp', Cc, prev_states) * jnp.exp(A_cs).transpose(0, 2, 3, 1)[..., None]
    y = (y_diag + y_off).reshape(bsz, L, SSD_HEADS, SSD_HEADDIM) + xs * d_skip.astype(f32)[:, None]
    y = y.reshape(bsz, L, SSD_INNER) * jax.nn.silu(z.astype(f32))
    y = rms_norm(y.reshape(bsz, L, SSD_NORM_GROUPS, SSD_INNER // SSD_NORM_GROUPS),
                 norm_w.reshape(SSD_NORM_GROUPS, SSD_INNER // SSD_NORM_GROUPS))
    return y.reshape(bsz, L, SSD_INNER).astype(z.dtype)

def hgrn2_mixer(q, f, i, g, lb, norm_w):
    bsz, L, _ = q.shape
    nc = L // CHUNK
    H, dk, dv = HGRN_HEADS, HGRN_KDIM, HGRN_VDIM
    qf = jax.nn.silu(q.astype(f32))
    ff = f.astype(f32)
    lbf = lb.astype(f32)
    kf = (1.0 - lbf) * jax.nn.sigmoid(-ff)
    log_forget = jnp.log1p(-kf)
    vf = i.astype(f32)

    def to_chunks(t, d):
        return t.reshape(bsz, nc, CHUNK, H, d).transpose(1, 0, 3, 2, 4)

    xs = (to_chunks(qf, dk), to_chunks(kf, dk), to_chunks(vf, dv), to_chunks(log_forget, dk))
    causal = jnp.tril(jnp.ones((CHUNK, CHUNK), bool))[None, None, :, :, None]

    def step(S, inp):
        qc, kc, vc, lf = inp
        b = jnp.cumsum(lf, axis=2)
        o_inter = jnp.einsum('bhtk,bhkv->bhtv', qc * jnp.exp(b), S)
        diff = b[:, :, :, None, :] - b[:, :, None, :, :]
        decay = jnp.where(causal, jnp.exp(jnp.where(causal, diff, 0.0)), 0.0)
        att = jnp.einsum('bhtk,bhsk,bhtsk->bhts', qc, kc, decay)
        o_intra = jnp.einsum('bhts,bhsv->bhtv', att, vc)
        b_last = b[:, :, -1]
        S_new = jnp.exp(b_last)[..., None] * S + jnp.einsum(
            'bhsk,bhsv->bhkv', kc * jnp.exp(b_last[:, :, None] - b), vc)
        return S_new, o_inter + o_intra

    S0 = jnp.zeros((bsz, H, dk, dv), f32)
    _, o = lax.scan(step, S0, xs)
    o = o.transpose(1, 0, 3, 2, 4).reshape(bsz, L, H, dv)
    o = rms_norm(o, norm_w) * jax.nn.silu(g.astype(f32).reshape(bsz, L, H, dv))
    return o.reshape(bsz, L, HGRN_VAL_WIDTH).astype(q.dtype)

def memory_attention(xq, mem, w_mem_kv):
    bsz, L, _ = xq.shape
    q = xq.reshape(bsz, L, MEM_HEADS, MEM_HEAD_DIM)
    kv = mem @ w_mem_kv
    k = kv[..., :MEM_WIDTH].reshape(bsz, -1, MEM_HEADS, MEM_HEAD_DIM)
    v = kv[..., MEM_WIDTH:].reshape(bsz, -1, MEM_HEADS, MEM_HEAD_DIM)
    s = jnp.einsum('blhd,bmhd->bhlm', q, k).astype(f32) * (MEM_HEAD_DIM ** -0.5)
    p = jax.nn.softmax(s, axis=-1).astype(v.dtype)
    return jnp.einsum('bhlm,bmhd->blhd', p, v).reshape(bsz, L, MEM_WIDTH)

def moe_ffn(h, w_router, router_bias, w_gate, w_up, w_down, ws_gate, ws_up, ws_down):
    N, D = h.shape
    E = N_EXPERTS
    scores = jax.nn.sigmoid((h @ w_router).astype(f32))
    choice = scores + router_bias.astype(f32)
    grp_score = lax.top_k(choice.reshape(N, N_GROUPS, E // N_GROUPS), 2)[0].sum(-1)
    _, gidx = lax.top_k(grp_score, TOPK_GROUPS)
    gmask = jax.nn.one_hot(gidx, N_GROUPS, dtype=f32).sum(1)
    emask = jnp.repeat(gmask, E // N_GROUPS, axis=1) > 0
    _, eidx = lax.top_k(jnp.where(emask, choice, MASK_SCORE), TOP_K)
    wts = jnp.take_along_axis(scores, eidx, axis=1)
    wts = wts / jnp.sum(wts, -1, keepdims=True) * ROUTED_SCALE
    NK = N * TOP_K
    NB = -(-NK // EXPERT_BLOCK) + E
    R = NB * EXPERT_BLOCK
    flat_e = eidx.reshape(NK)
    flat_tok = jnp.repeat(jnp.arange(N, dtype=jnp.int32), TOP_K)
    flat_w = wts.reshape(NK)
    order = jnp.argsort(flat_e)
    se = flat_e[order]
    counts = jnp.bincount(flat_e, length=E)
    starts = jnp.cumsum(counts) - counts
    rank = jnp.arange(NK) - starts[se]
    padded = (counts + EXPERT_BLOCK - 1) // EXPERT_BLOCK * EXPERT_BLOCK
    pend = jnp.cumsum(padded)
    dest = (pend - padded)[se] + rank
    row_tok = jnp.zeros((R,), jnp.int32).at[dest].set(flat_tok[order])
    row_w = jnp.zeros((R,), f32).at[dest].set(flat_w[order])
    block_e = jnp.minimum(jnp.searchsorted(pend, jnp.arange(NB) * EXPERT_BLOCK, side='right'), E - 1)

    def expert_block(args):
        e, tok, wr = args
        xb = h[tok]
        y = (jax.nn.silu(xb @ w_gate[e]) * (xb @ w_up[e])) @ w_down[e]
        return y * wr[:, None].astype(h.dtype)

    ys = lax.map(expert_block, (block_e, row_tok.reshape(NB, EXPERT_BLOCK), row_w.reshape(NB, EXPERT_BLOCK)))
    routed = jax.ops.segment_sum(ys.reshape(R, D), row_tok, num_segments=N)
    shared = (jax.nn.silu(h @ ws_gate) * (h @ ws_up)) @ ws_down
    return routed + shared

def hgrn_lower_bounds(lb_param):
    sm = jax.nn.softmax(lb_param.astype(f32), axis=0)
    return jnp.cumsum(sm, axis=0) - sm[0:1]

def setup_inputs(seed: int = 0) -> dict:
    key = jax.random.key(seed)
    ks = iter(jax.random.split(key, 40))

    def nrm(shape, scale):
        return jax.random.normal(next(ks), shape, f32) * scale

    dt0 = jnp.exp(jax.random.uniform(next(ks), (DEPTH, SSD_HEADS), f32)
                  * (math.log(0.1) - math.log(0.001)) + math.log(0.001))
    return {
        "x": nrm((BATCH, SEQ, D_MODEL), 1.0),
        "mem": nrm((BATCH, MEM_TOKENS, D_MODEL), 1.0),
        "w_in": nrm((DEPTH, D_MODEL, IN_COLS), D_MODEL ** -0.5),
        "conv_w": nrm((DEPTH, SSD_CONV, SSD_CONV_DIM), SSD_CONV ** -0.5),
        "conv_b": nrm((DEPTH, SSD_CONV_DIM), 0.02),
        "dt_bias": dt0 + jnp.log(-jnp.expm1(-dt0)),
        "a_log": jnp.log(jax.random.uniform(next(ks), (DEPTH, SSD_HEADS), f32, 1.0, 16.0)),
        "d_skip": 1.0 + nrm((DEPTH, SSD_HEADS), 0.1),
        "ssd_norm": 1.0 + nrm((DEPTH, SSD_INNER), 0.02),
        "pool_w": nrm((DEPTH, len(POOL_WINDOWS), POOL_GROUP, POOL_GROUP), POOL_GROUP ** -0.5),
        "pool_scale": 1.0 + nrm((DEPTH, POOL_WIDTH), 0.02),
        "hgrn_lb": nrm((DEPTH, HGRN_KEY_WIDTH), 0.1),
        "hgrn_norm": 1.0 + nrm((DEPTH, HGRN_VDIM), 0.02),
        "w_mem_kv": nrm((DEPTH, D_MODEL, 2 * MEM_WIDTH), D_MODEL ** -0.5),
        "w_branch": nrm((DEPTH, N_BRANCH, BRANCH_WIDTH, D_MODEL), BRANCH_WIDTH ** -0.5),
        "w_o": nrm((DEPTH, D_MODEL, D_MODEL), D_MODEL ** -0.5 * BETA),
        "ln1_g": 1.0 + nrm((DEPTH, D_MODEL), 0.02),
        "ln1_b": nrm((DEPTH, D_MODEL), 0.02),
        "w_router": nrm((DEPTH, D_MODEL, N_EXPERTS), D_MODEL ** -0.5),
        "router_bias": nrm((DEPTH, N_EXPERTS), 0.01),
        "w_exp_gate": nrm((DEPTH, N_EXPERTS, D_MODEL, D_EXPERT), D_MODEL ** -0.5),
        "w_exp_up": nrm((DEPTH, N_EXPERTS, D_MODEL, D_EXPERT), D_MODEL ** -0.5),
        "w_exp_down": nrm((DEPTH, N_EXPERTS, D_EXPERT, D_MODEL), D_EXPERT ** -0.5 * BETA),
        "w_sh_gate": nrm((DEPTH, D_MODEL, D_SHARED), D_MODEL ** -0.5),
        "w_sh_up": nrm((DEPTH, D_MODEL, D_SHARED), D_MODEL ** -0.5),
        "w_sh_down": nrm((DEPTH, D_SHARED, D_MODEL), D_SHARED ** -0.5 * BETA),
        "ln2_g": 1.0 + nrm((DEPTH, D_MODEL), 0.02),
        "ln2_b": nrm((DEPTH, D_MODEL), 0.02),
    }

def reference(x, mem, w_in, conv_w, conv_b, dt_bias, a_log, d_skip, ssd_norm, pool_w, pool_scale,
              hgrn_lb, hgrn_norm, w_mem_kv, w_branch, w_o, ln1_g, ln1_b, w_router, router_bias,
              w_exp_gate, w_exp_up, w_exp_down, w_sh_gate, w_sh_up, w_sh_down, ln2_g, ln2_b):
    bsz, L, D = x.shape
    lb_all = hgrn_lower_bounds(hgrn_lb)
    split_at = np.cumsum(IN_SPLITS)[:-1].tolist()
    h = x
    for l in range(DEPTH):
        proj = h @ w_in[l]
        (u_pool, z_ssd, xbc_ssd, dt_ssd, q_h, f_h, i_h, g_h, q_mem, gate_logits) = jnp.split(proj, split_at, axis=-1)
        branches = (
            pool_mixer(u_pool, pool_w[l], pool_scale[l]),
            ssd_mixer(z_ssd, xbc_ssd, dt_ssd, conv_w[l], conv_b[l], dt_bias[l], a_log[l], d_skip[l], ssd_norm[l]),
            hgrn2_mixer(q_h, f_h, i_h, g_h, lb_all[l], hgrn_norm[l]),
            memory_attention(q_mem, mem, w_mem_kv[l]),
        )
        gates = jax.nn.sigmoid(gate_logits.astype(f32)).reshape(bsz, L, N_BRANCH, D).astype(h.dtype)
        merged = gates[:, :, 0] * (branches[0] @ w_branch[l, 0])
        for n in range(1, N_BRANCH):
            merged = merged + gates[:, :, n] * (branches[n] @ w_branch[l, n])
        h = layer_norm(ALPHA * h + merged @ w_o[l], ln1_g[l], ln1_b[l])
        ff = moe_ffn(h.reshape(bsz * L, D), w_router[l], router_bias[l], w_exp_gate[l], w_exp_up[l],
                     w_exp_down[l], w_sh_gate[l], w_sh_up[l], w_sh_down[l]).reshape(bsz, L, D)
        h = layer_norm(ALPHA * h + ff, ln2_g[l], ln2_b[l])
    return h


_drawn_inputs = setup_inputs


def setup_inputs(seed=0):
    import zlib

    import numpy as np

    out = dict(_drawn_inputs(seed))
    spreads = {}
    factors = {'ssd_norm': 3.401, 'hgrn_norm': 3.926, 'ln2_g': 8.397, 'ln2_b': 8.187, 'pool_scale': 2.893}
    for name, (base, spread) in spreads.items():
        noise = np.random.default_rng([zlib.crc32(name.encode()), seed]).standard_normal(out[name].shape)
        drawn = base * np.exp(spread * noise) if base else spread * noise
        out[name] = __import__('jax').numpy.asarray(drawn.astype(out[name].dtype))
    for name, factor in factors.items():
        out[name] = (out[name] * factor).astype(out[name].dtype)
    return out
```

```python
import concourse.bass as bass
from concourse import mybir
from concourse.alu_op_type import AluOpType as ALU

f32 = mybir.dt.float32
f32r = mybir.dt.float32r
i32 = mybir.dt.int32
u8 = mybir.dt.uint8
ACT = mybir.ActivationFunctionType
AX = mybir.AxisListType

P = 128
D = 2048
S = 256
TT = S // P
KT = D // P
PARTS = 4
UK, UC = 8, 256
HALVES = 9
POOL, QMEM, FGT, QRY, XS, BC, OGATE, VAL, ZG = range(HALVES)
UP = 2 * HALVES
DBLK = D // UC
UM = 12
N_X = 4
N_KV = 16
N_P0 = N_X + N_KV
N_M0 = N_P0 + PARTS * UP
N_O0 = N_M0 + DBLK * UM
N_S0 = N_O0 + 2 * DBLK
N_D0 = N_S0 + 4
N_UNITS = N_D0 + 2
START = 1
RAW, SPLIT = 3, 2

E = 64
TOPK, GROUPS, TOPG = 8, 8, 4
PAIRS = E // 2
CAP = 64
ROUTED_SCALE = 2.5
MASK_SCORE = -1e4
FE = 256
ALPHA = 2.0 ** 0.25
EPS = 1e-5
LEVELS = 9
NP = 28


def build_trunk(nc, units, params, hnorm, wdt, dtb, alog, poolm, poolw, xtok, lnp, wrt, rbias, wgu, wd, out):
    base = 16512

    def at(name, kb, shape, dt=f32):
        return nc.alloc_sbuf_tensor_at(name, shape, dt, offset=base + int(kb * 1024))

    xhi = at("xhi", 0, [P, KT, S], f32r)
    xlo = at("xlo", 16, [P, KT, S], f32r)
    raw = [at(f"raw{s}", 32 + 8 * s, [P, UK * UC]) for s in range(RAW)]
    whi = [at(f"whi{s}", 56 + 8 * s, [P, UK * UC], f32r) for s in range(SPLIT)]
    wlo = [at(f"wlo{s}", 72 + 8 * s, [P, UK * UC], f32r) for s in range(SPLIT)]
    ident = at("ident", 88, [P, P])
    later = at("later", 88.5, [P, P])
    upto = at("upto", 89, [P, P])
    before = at("before", 89.5, [P, P])
    ones = at("ones", 90, [P, P])
    quart = at("quart", 90.5, [P, 3, P])
    lmask = at("lmask", 92, [P, LEVELS - 2, P], u8)
    par = at("par", 93, [P, PARTS, NP])
    prm = at("prm", 93.5, [P, NP])
    hnw = at("hnw", 93.8125, [P, 8])
    hdt = at("hdt", 93.875, [P, TT, 16])
    ad = at("ad", 94, [P, TT, 16])
    small = at("small", 94.25, [P, 16, 8])
    kT = at("kT", 96, [P, 8, S])
    vmem = at("vmem", 104, [P, TT, 4 * UC])
    yT = at("yT", 112, [P, 4, 8, S])
    mhi = at("mhi", 144, [P, KT, S], f32r)
    mlo = at("mlo", 160, [P, KT, S], f32r)
    tok = [0.0]

    def tmp(name, shape, dt=f32, start=144):
        n = 1
        for d in shape[1:]:
            n *= d
        t = at(name, start + tok[0], shape, dt)
        tok[0] += (n * 4 + 31) // 32 * 32 / 1024
        assert start + tok[0] <= 207.8, (name, tok[0])
        return t

    poolmix = tmp("poolmix", [P, TT, S])
    poolwt = tmp("poolwt", [P, 2, UC])
    upool = tmp("upool", [P, TT, UC])
    dpool = tmp("dpool", [P, 2, S])
    qm = tmp("qm", [P, 2, S])
    vm = tmp("vm", [P, 2, UC])
    prob = tmp("prob", [P, TT, S])
    probT = tmp("probT", [P, 2, S])
    fgate = tmp("fgate", [P, 2 * S])
    fr = tmp("fr", [P, 2, S])
    kk = tmp("kk", [P, 2, S])
    qq = tmp("qq", [P, 2, S])
    blk = [fgate, tmp("blk2", [P, S])] + [tmp(f"blk{2 ** j}", [P, S >> (j - 1)]) for j in range(2, 8)]
    att = tmp("att", [P, 2 * TT, P])
    attx = tmp("attx", [P, 2, P])
    vh = tmp("vh", [P, TT, UC])
    gs = tmp("gs", [P, 2, S])
    th = tmp("th", [P, 2, S])
    up = tmp("up", [P, 4, 3 + S])
    cv = tmp("cv", [P, 4, S])
    tc = tmp("tc", [P, 4, S])
    xt = tmp("xt", [P, TT, UC])
    dec = tmp("dec", [P, 3, 4, P])
    ta = tmp("ta", [P, 3, 4, P])
    cbm = tmp("cbm", [P, 3, P])
    osq, rh, rs = th[:, :, :].rearrange("p a b -> p (a b)"), kk[:, :, :].rearrange("p a b -> p (a b)"), blk[1]
    zs, yss = fr, qq
    wdt_raw = at("wdt_raw", 176, [P, KT * 16])
    wdt_hi = at("wdt_hi", 177, [P, KT, 16], f32r)
    wdt_lo = at("wdt_lo", 178, [P, KT, 16], f32r)
    dtbias = at("dtbias", 179, [P, 32])
    aneg = at("aneg", 179.25, [P, 32])
    dts = at("dts", 179.5, [P, 8, 32])
    xi = at("xi", 181, [P, 2 * P], i32)
    xf = at("xf", 182, [P, 3, P])
    N_CONST = 14

    yhi = [at(f"yhi{n}", o, [P, UK, S], f32r) for n, o in enumerate((96, 144, 160, 176))]
    ylo = [at(f"ylo{n}", o + 8, [P, UK, S], f32r) for n, o in enumerate((96, 144, 160, 176))]
    ghi = at("merged_hi", 112, [P, KT, S], f32r)
    glo = at("merged_lo", 128, [P, KT, S], f32r)
    sig = at("sig", 192, [P, 4, 2 * S])
    macc = at("macc", 200, [P, 2 * S])
    mtmp = at("mtmp", 202, [P, 2 * S])
    htok = at("h", 144, [P, TT, D])
    lng = [at("ln1_gain", 176, [P, D]), at("ln2_gain", 64, [P, D])]
    lnb = [at("ln1_bias", 184, [P, D]), at("ln2_bias", 72, [P, D])]
    bns = at("bns", 204, [P, TT, 4, 6])
    bna = at("bna", 204.25, [P, TT, 2])
    bnr = at("bnr", 204.5, [P, TT, 4])
    wrt_raw = at("wrt_raw", 192, [P, KT, E])
    wrt_st = at("wrt_stacked", 196, [P, KT, 2 * E], f32r)
    stack_id = at("stack_id", 120, [P, E])
    rsum = at("rsum", 120.5, [P, S])
    sth = at("sth", 112, [P, 2 * S])
    sact = at("sact", 114, [P, 2 * S])
    shi = at("shi", 116, [P, 2, S], f32r)
    slo = at("slo", 118, [P, 2, S], f32r)
    EE = [P, TT, E]
    score, choice, masked, repl, sel, wsel, rtmp = (at(f"router{j}", 121.5 + j * 0.5, EE) for j in range(7))
    gmax = at("gmax", 125, [P, TT, GROUPS, 8])
    gsum = at("gsum", 125.5, [P, TT, GROUPS])
    gcmp = at("gcmp", 125.75, [P, TT, GROUPS, GROUPS])
    gcmp2 = at("gcmp2", 126.25, [P, TT, GROUPS, GROUPS])
    gmask = at("gmask", 126.75, [P, TT, GROUPS])
    gpen = at("gpen", 127, [P, TT, GROUPS])
    top8 = at("top8", 127.25, [P, TT, 8])
    wsum = at("wsum", 127.5, [P, TT, 2])
    rbias_t = at("router_bias", 95.25, [P, E])
    glt = at("group_before", 95, [P, GROUPS, GROUPS])
    acc = at("acc", 128, [P, TT, D])
    EP = E + 4
    rank = at("rank", 205.5, [P, TT, EP])
    wgt = at("wgt", 206.25, [P, TT, EP])
    slots = at("slots", 94.75, [P, CAP])
    rounds = at("rounds", 207.25, [P, 1], i32)
    rcnt = at("rcnt", 207.3125, [P, 4])
    wgu_t = [at("wgu0", 96, [P, 4, 4, 2 * FE]), at("wgu1", 0, [P, 4, 4, 2 * FE])]
    wd_t = [at("wd0", 160, [P, 2, D]), at("wd1", 176, [P, 2, D])]
    xg = at("xg", 32, [P, KT, 2 * CAP])
    ye = at("ye", 40, [P, D])
    pick = at("pick", 56, [P, TT, 2, CAP])
    pickw = at("pickw", 57, [P, TT, 2, CAP])
    pickT = at("pickT", 58, [P, TT, P])
    eth = at("eth", 59, [P, FE])
    eact = at("eact", 60, [P, FE])
    eactT = at("eactT", 61, [P, 2, P])

    bank = [nc.alloc_psum_tensor(f"bank{b}", [P, 512], f32) for b in range(8)]

    def sem(name):
        return nc.alloc_semaphore(name)

    raw_full = [sem(f"raw_full{s}") for s in range(RAW)]
    hi_done, lo_done, unit_used = sem("hi_done"), sem("lo_done"), sem("unit_used")
    par_in, const_ok, dt_in = sem("par_in"), sem("const_ok"), sem("dt_in")
    mem_read = sem("mem_read")
    lb_e, lb_x = sem("lb_ready"), sem("lb_exp")

    NH = 8

    def cnt(i, per, k):
        return i * per + k

    def half_count(p, h):
        return p * UP + (N_KV + 2 * h)

    def dense(pe, n, u, out_bank, act_hi, act_lo, kofs, first, last, tokens_stationary):
        hi, lo = whi[u % SPLIT], wlo[u % SPLIT]
        pe.wait_ge(lo_done, n + 1)
        m = None
        for t in range(2):
            for k in range(UK):
                wh, wl = (w[:, k * UC:(k + 1) * UC] for w in (hi, lo))
                xh, xl = act_hi[:, kofs + k, :], act_lo[:, kofs + k, :]
                for j, (w, x) in enumerate(((wh, xh), (wh, xl), (wl, xh))):
                    if tokens_stationary:
                        lhsT, rhs = x[:, t * P:(t + 1) * P], w
                    else:
                        lhsT, rhs = w[:, t * P:(t + 1) * P], x
                    m = nc.tensor.matmul(out_bank[:, t * UC:(t + 1) * UC], lhsT, rhs,
                                         start=first and t == 0 and k == 0 and j == 0,
                                         stop=last and k == UK - 1 and j == 2, skip_group_check=True)
        m.then_inc(unit_used, 1)
        return m

    def split_hi(act, n, u, dst=None):
        act.wait_ge(raw_full[u % RAW], (n // RAW + 1) * 16 if isinstance(n, int) else n)
        return nc.scalar.activation(whi[u % SPLIT][:, :] if dst is None else dst, raw[u % RAW][:, :], ACT.Copy)

    names = ("u_ok pmix_in pw_in dp_ps dp_ok yp_ps yp_ok qm_ok vm_ok sc_ps nmx_ok p_ok pn_ok pt_ps pt_ok cx_ps cx_ok "
             "f_exp kk_ok qt_ok lev_ps lev_ok lev_k x_ps x_ok vh_ok gt_ok gs_ok o_ps osq_ok oss_ps ovar_ok osd_ok yh_ok "
             "up_ok cv_ok tc_ok xc_ok xtp_ps xt_ok cb_ps cb_ok ta_ok dec_ps dec_ok g_ok y_ps tz_ok y1_ok ysq_ok "
             "yss_ps yvar_ok ysd_ok ys_ok vch").split()
    s = {n: sem("part_" + n) for n in names}
    dt_ps, dt_e, dt_l, dt_a, dt_w = sem("dt_ps"), sem("dt_e"), sem("dt_l"), sem("dt_a"), sem("dt_w")
    upz = sem("up_zeroed")
    dt_chain = sem("dt_chain")
    mg = {n: sem("merge_" + n) for n in "y_hi y_lo gate_ok mul_ok block_ok ch".split()}
    og = {n: sem("out_" + n) for n in
         "x_in res_ok ln_in stats_ok sd_ok nrm_ok scaled_ok tr_ps hi_ok lo_ok ln_ch w_in whi_ok wlo_ok".split()}
    rt = {n: sem("router_" + n) for n in "ps sum_ok lg_ps exp_ok sel_ok rk_ps ch rounds_ok ready".split()}
    sh = {n: sem("shared_" + n) for n in "th_ok a_ok hi_ok lo_ok acc_ok ch dps".split()}
    ex = {n: sem("expert_" + n) for n in
         "gu_free pick_ok pickw_ok ga_ps xg_act xg_dve gu_ps th_ok a_ok ch at_ps at_ok pt_ps pt_ok y_ps y_ok "
         "sc_ps acc_ok zero round_end out_ok g2".split()}
    gu_full = [sem(f"expert_gu_full{c}") for c in range(4)]
    d_full = [sem(f"expert_d_full{c}") for c in range(2)]
    VC = 35

    def unit_wait(i, per, b, u):
        assert (b + u) % RAW == (b + u) % RAW and per % RAW == 0
        return (i * (per // RAW) + (b + u) // RAW + 1) * 16

    blkctx = nc.Block()
    block = blkctx.__enter__()

    @block.sync
    def _(sp):
        for u in range(RAW):
            sp.dma_start(raw[u][:, :], units[u]).then_inc(raw_full[u], 16)
        sp.dma_start(wdt_raw[:, :], wdt).then_inc(dt_in, 16)
        sp.dma_start(par[:, :, :], params).then_inc(par_in, 16)
        sp.dma_start(hnw[:, 0:1], hnorm).then_inc(par_in, 16)
        sp.dma_start(dtbias[:, :], dtb).then_inc(par_in, 16)
        sp.dma_start(aneg[:, :], alog).then_inc(par_in, 16)
        with sp.Fori(1, N_UNITS // RAW) as r:
            for u in range(RAW):
                sp.wait_ge(hi_done, r * RAW + (u + 1 - RAW))
                sp.wait_ge(lo_done, r * RAW + (u + 1 - RAW))
                sp.dma_start(raw[u][:, :], units[r * RAW + u]).then_inc(raw_full[u], 16)

        def load_pair(it, pair):
            for c in range(4):
                for j in range(2):
                    sp.wait_ge(ex["gu_free"], it * 4 + (c + 1))
                    sp.dma_start(wgu_t[j][:, c, :, :], wgu[pair * 2 + j, c]).then_inc(gu_full[c], 16)
            for c in range(2):
                for j in range(2):
                    sp.wait_ge(ex["y_ps"], it * 4 + START)
                    sp.dma_start(wd_t[j][:, c, :], wd[pair * 2 + j, c]).then_inc(d_full[c], 16)

        with sp.Fori(0, PAIRS) as pair:
            load_pair(pair, pair)
        sp.wait_ge(rt["rounds_ok"], 1)
        n_rounds = sp.value_load(rounds[0:1, 0:1], min_val=1, max_val=4)
        with sp.If(n_rounds > 1):
            with sp.Fori(1, n_rounds) as b:
                with sp.Fori(0, PAIRS) as pair:
                    load_pair(b * PAIRS + pair, pair)
        for t in range(TT):
            sp.wait_ge(og["scaled_ok"], TT + t + 1)
            sp.dma_start(out[t * P:(t + 1) * P, :], acc[:, t, :]).then_inc(ex["out_ok"], 16)
        sp.wait_ge(ex["out_ok"], 16 * TT)

    started = [s[n] for n in "cv_ok cx_ps dec_ps dp_ps gs_ok kk_ok o_ps oss_ps p_ok pt_ps sc_ps vh_ok x_ok x_ps y1_ok "
                             "y_ps yh_ok yp_ps ys_ok yss_ps".split()]
    started += [mg[n] for n in "block_ok gate_ok mul_ok".split()] + [og["res_ok"]]
    started += [ex[n] for n in "a_ok acc_ok at_ps ga_ps pt_ok pt_ps xg_act xg_dve y_ok y_ps".split()]

    @block.gpsimd
    def _(pool):
        for one in started:
            pool.sem_inc(one, START)
        chain = [0]

        def link(ins):
            chain[0] += 1
            ins.then_inc(const_ok, 1)
            pool.wait_ge(const_ok, chain[0])

        link(nc.gpsimd.memset(ones[:, :], 1.0))
        link(nc.gpsimd.memset(ident[:, :], 0.0))
        link(nc.gpsimd.memset(quart[:, :, :], 0.25))
        link(nc.gpsimd.affine_select(out=ident[:, :], in_=ident[:, :], compare_op=ALU.not_equal, fill=1.0, base=0,
                                     pattern=[[-1, P]], channel_multiplier=1))
        link(nc.gpsimd.affine_select(out=later[:, :], in_=ones[:, :], compare_op=ALU.is_gt, fill=0.0, base=0,
                                     pattern=[[-1, P]], channel_multiplier=1))
        link(nc.gpsimd.affine_select(out=upto[:, :], in_=ones[:, :], compare_op=ALU.is_ge, fill=0.0, base=0,
                                     pattern=[[1, P]], channel_multiplier=-1))
        link(nc.gpsimd.affine_select(out=before[:, :], in_=ones[:, :], compare_op=ALU.is_gt, fill=0.0, base=0,
                                     pattern=[[1, P]], channel_multiplier=-1))
        for b in (0, 2):
            link(nc.gpsimd.affine_select(out=quart[:, b, :], in_=quart[:, b, :], compare_op=ALU.is_ge, fill=0.0,
                                         base=0, pattern=[[1, P]], channel_multiplier=-1))
        link(nc.gpsimd.iota(xi[:, 0:P], [[1, P]], base=0, channel_multiplier=0))
        link(nc.gpsimd.iota(xi[:, P:2 * P], [[0, P]], base=0, channel_multiplier=1))
        link(nc.gpsimd.iota(slots[:, :], [[1, CAP]], base=0, channel_multiplier=0, allow_small_or_imprecise_dtypes=True))
        link(nc.gpsimd.memset(glt[:, :, :], 1.0))
        link(nc.gpsimd.affine_select(out=glt[:, :, :], in_=glt[:, :, :], compare_op=ALU.is_gt, fill=0.0, base=0,
                                     pattern=[[1, GROUPS], [-1, GROUPS]], channel_multiplier=0))
        assert chain[0] == N_CONST
        with pool.Fori(0, PARTS) as p:
            pool.wait_ge(s["cx_ps"], p + START)
            pool.wait_ge(mem_read, NH)
            pool.wait_ge(unit_used, 2 * NH)
            nc.gpsimd.tensor_copy(vm[:, :, :], vmem[:, :, bass.ts(p, UC)]).then_inc(s["vm_ok"], 1)

        pool.dma_start(rbias_t[:, :], rbias.partition_broadcast(P)).then_inc(og["w_in"], 16)
        pool.wait_ge(mg["block_ok"], DBLK + START)
        pool.wait_ge(unit_used, N_O0 - N_X)
        for t in range(TT):
            pool.dma_start(htok[:, t, :], xtok[t * P:(t + 1) * P, :]).then_inc(og["x_in"], 16)
        pool.dma_start(wrt_raw[:, :, :], wrt).then_inc(og["w_in"], 16)
        pool.dma_start(lng[0][:, :], lnp[0].partition_broadcast(P)).then_inc(og["ln_in"], 16)
        pool.dma_start(lnb[0][:, :], lnp[1].partition_broadcast(P)).then_inc(og["ln_in"], 16)
        pool.wait_ge(unit_used, N_UNITS - N_X)
        pool.dma_start(lng[1][:, :], lnp[2].partition_broadcast(P)).then_inc(ex["g2"], 16)
        pool.dma_start(lnb[1][:, :], lnp[3].partition_broadcast(P)).then_inc(ex["g2"], 16)

    @block.tensor
    def _(pe):
        pe.wait_ge(lo_done, N_X)
        pe.wait_ge(const_ok, N_CONST)
        pe.wait_ge(dt_w, 2)
        for t in range(TT):
            for k in range(KT):
                for j, (x, w) in enumerate(((xhi, wdt_hi), (xlo, wdt_hi), (xhi, wdt_lo))):
                    m = nc.tensor.matmul(bank[7][:, 16 * t:16 * t + 16], x[:, k, t * P:(t + 1) * P], w[:, k, :],
                                         start=k == 0 and j == 0, stop=k == KT - 1 and j == 2)
        m.then_inc(dt_ps, 1)
        for h in range(NH):
            if h >= 3:
                pe.wait_ge(mem_read, h - 2)
            for j in range(2):
                n = N_X + 2 * h + j
                m = dense(pe, n, n, bank[h % 3], mhi, mlo, UK * j, j == 0, j == 1, h >= 4)
        pe.wait_ge(mem_read, NH)
        with pe.Fori(0, PARTS) as p:
            def half(h, j):
                n = N_P0 + 2 * h + j
                if j == 0:
                    if h == 0:
                        pe.wait_ge(s["gs_ok"], p + START)
                    elif h == 1:
                        pe.wait_ge(s["vh_ok"], p + START)
                    elif h == 2:
                        pe.wait_ge(s["y1_ok"], p + START)
                    elif h == 3:
                        pe.wait_ge(s["u_ok"], p + 1)
                    elif h == 4:
                        pe.wait_ge(s["qm_ok"], p + 1)
                    elif h == 5:
                        pe.wait_ge(s["f_exp"], p + 1)
                    elif h == 6:
                        pe.wait_ge(s["lev_ok"], cnt(p, 17, 1))
                    elif h == 7:
                        pe.wait_ge(s["up_ok"], cnt(p, 2, 1))
                    elif h == 8:
                        pe.wait_ge(s["up_ok"], cnt(p, 2, 2))
                m = dense(pe, p * UP + n, n, bank[h % 3], xhi, xlo, UK * j, j == 0, j == 1, h in (POOL, VAL))

            def mm(o, a, b, start=True, stop=True, **kw):
                return nc.tensor.matmul(o, a, b, start=start, stop=stop, **kw)

            def level(l):
                if l == 0:
                    pe.wait_ge(s["kk_ok"], p + 1 + START)
                    pe.wait_ge(s["x_ok"], p + START)
                pe.wait_ge(s["lev_ok"], cnt(p, 17, 2 * l + 1))
                for h in range(2):
                    if l < LEVELS - 1:
                        for t in range(TT):
                            sl = slice(t * P, (t + 1) * P)
                            m = mm(bank[6][:, (2 * h + t) * P:(2 * h + t + 1) * P], kk[:, h, sl], qq[:, h, sl])
                    else:
                        m = mm(bank[6][:, h * P:(h + 1) * P], kk[:, h, 0:P], qq[:, h, P:S])
                m.then_inc(s["lev_ps"] if l < LEVELS - 1 else s["x_ps"], 1)

            half(0, 0)
            half(0, 1)
            pe.wait_ge(s["ta_ok"], 3 * p + 3)
            pe.wait_ge(s["y1_ok"], p + START)
            mm(bank[5][:, :], later[:, :], ta[:, 0, :, :].rearrange("p h l -> p (h l)")).then_inc(s["dec_ps"], 1)
            half(1, 0)
            pe.wait_ge(s["dec_ok"], cnt(p, 3, 1))
            mm(bank[5][:, :], later[:, :], ta[:, 1, :, :].rearrange("p h l -> p (h l)")).then_inc(s["dec_ps"], 1)
            half(1, 1)
            pe.wait_ge(s["dec_ok"], cnt(p, 3, 2))
            mm(bank[5][:, :], later[:, :], ta[:, 2, :, :].rearrange("p h l -> p (h l)"), stop=False)
            mm(bank[5][:, :], ones[:, :], ta[:, 1, :, :].rearrange("p h l -> p (h l)"), start=False)\
                .then_inc(s["dec_ps"], 1)
            pe.wait_ge(s["u_ok"], p + 1)
            pe.wait_ge(s["pmix_in"], (p + 1) * 16)
            pe.wait_ge(s["yh_ok"], p + START)
            for c in range(2):
                for t in range(TT):
                    m = mm(bank[3][:, c * S:(c + 1) * S], upool[:, t, c * P:(c + 1) * P], poolmix[:, t, :],
                           t == 0, t == TT - 1)
            m.then_inc(s["dp_ps"], 1)
            half(2, 0)
            half(2, 1)
            pe.wait_ge(s["dp_ok"], p + 1)
            pe.wait_ge(s["pw_in"], (p + 1) * 16)
            pe.wait_ge(s["ys_ok"], 2 * p + START)
            for c in range(2):
                for k in range(2):
                    m = mm(bank[4][:, c * S:(c + 1) * S], poolwt[:, k, c * P:(c + 1) * P], dpool[:, k, :],
                           k == 0, k == 1)
            m.then_inc(s["yp_ps"], 1)
            pe.wait_ge(s["qm_ok"], p + 1)
            for t in range(TT):
                for k in range(2):
                    m = mm(bank[3][:, t * S:(t + 1) * S], qm[:, k, t * P:(t + 1) * P], kT[:, p * 2 + k, :],
                           k == 0, k == 1)
            m.then_inc(s["sc_ps"], 1)
            half(3, 0)
            half(3, 1)
            half(4, 0)
            level(0)
            half(4, 1)
            level(1)
            pe.wait_ge(s["pn_ok"], p + 1)
            pe.wait_ge(s["yp_ok"], 2 * p + 2)
            for mt in range(2):
                for t in range(TT):
                    m = nc.tensor.transpose(bank[4][:, mt * S + t * P:mt * S + (t + 1) * P],
                                            prob[:, t, mt * P:(mt + 1) * P], ident[:, :])
            m.then_inc(s["pt_ps"], 1)
            half(5, 0)
            level(2)
            half(5, 1)
            level(3)
            pe.wait_ge(s["pt_ok"], p + 1)
            pe.wait_ge(s["vm_ok"], p + 1)
            for c in range(2):
                for mt in range(2):
                    m = mm(bank[3][:, c * S:(c + 1) * S], vm[:, mt, c * P:(c + 1) * P], probT[:, mt, :],
                           mt == 0, mt == 1)
            m.then_inc(s["cx_ps"], 1)
            half(6, 0)
            level(4)
            half(6, 1)
            level(5)
            pe.wait_ge(s["xc_ok"], cnt(p, 2, 1))
            for t in range(TT):
                for c in range(2):
                    m = nc.tensor.transpose(bank[4][:, t * UC + c * P:t * UC + (c + 1) * P],
                                            cv[:, c, t * P:(t + 1) * P], ident[:, :])
            m.then_inc(s["xtp_ps"], 1)
            half(7, 0)
            level(6)
            pe.wait_ge(s["xc_ok"], cnt(p, 2, 2))
            pe.wait_ge(s["cx_ok"], p + 1)
            mm(bank[3][:, 0:S], cv[:, 2, 0:P], cv[:, 3, :])
            mm(bank[3][:, S:S + P], cv[:, 2, P:S], cv[:, 3, P:S]).then_inc(s["cb_ps"], 1)
            half(7, 1)
            level(7)
            half(8, 0)
            level(8)
            half(8, 1)
            pe.wait_ge(s["g_ok"], p + 1)
            pe.wait_ge(s["xt_ok"], 2 * p + 2)
            for c in range(2):
                for (l, terms) in ((0, ((0, 0),)), (1, ((0, 1), (1, 2)))):
                    for i, (t, b) in enumerate(terms):
                        for r in range(2):
                            h = 2 * c + r
                            m = mm(bank[5][64 * r:64 * r + 64, c * S + l * P:c * S + (l + 1) * P],
                                   xt[:, t, 64 * h:64 * h + 64], dec[:, b, h, :], i == 0, i == len(terms) - 1)
            m.then_inc(s["y_ps"], 1)
            pe.wait_ge(s["x_ok"], p + 1 + START)
            pe.wait_ge(s["vh_ok"], p + 1 + START)
            pe.wait_ge(s["lev_ok"], cnt(p, 17, 17))
            for h in range(2):
                vs = [vh[:, t, h * P:(h + 1) * P] for t in range(TT)]
                mm(bank[7][:, h * S:h * S + P], vs[0], att[:, 2 * h, :])
                mm(bank[7][:, h * S + P:(h + 1) * S], vs[1], att[:, 2 * h + 1, :], stop=False)
                m = mm(bank[7][:, h * S + P:(h + 1) * S], vs[0], attx[:, h, :], start=False)
            m.then_inc(s["o_ps"], 1)
            pe.wait_ge(s["osq_ok"], p + 1)
            pe.wait_ge(s["cb_ok"], p + 1)
            mm(bank[3][:, :], ones[:, :], osq).then_inc(s["oss_ps"], 1)
            pe.wait_ge(s["ysq_ok"], p + 1)
            mm(bank[4][:, 0:S], ones[:, :], tc[:, 0, :], stop=False)
            mm(bank[4][:, 0:S], ones[:, :], tc[:, 1, :], start=False).then_inc(s["yss_ps"], 1)


        pe.wait_ge(s["ys_ok"], 2 * PARTS + START)
        pe.wait_ge(s["yh_ok"], PARTS + START)
        pe.wait_ge(s["yp_ok"], 2 * PARTS)
        pe.wait_ge(s["cx_ok"], PARTS)
        pe.wait_ge(mg["y_lo"], 4)
        with pe.Fori(0, DBLK) as b:
            for n in range(4):
                for j in range(2):
                    u = 3 * n + j
                    if n == 0 and j == 0:
                        pe.wait_ge(mg["gate_ok"], b * 4 + START)
                    dense(pe, b * UM + (N_M0 + u), N_M0 + u, bank[2 * n], xhi, xlo, UK * j, j == 0, j == 1, False)
                if n == 0:
                    pe.wait_ge(mg["mul_ok"], b * 4 + START)
                u = 3 * n + 2
                dense(pe, b * UM + (N_M0 + u), N_M0 + u, bank[2 * n + 1], yhi[n], ylo[n], 0, True, True, False)

        pe.wait_ge(mg["block_ok"], DBLK + START)
        pe.wait_ge(mg["gate_ok"], 4 * DBLK + START)

        def out_half(i, c, u0):
            for j in range(2):
                dense(pe, i + (N_O0 + u0 + j), N_O0 + u0 + j, bank[u0 // 2 % 3], ghi, glo, UK * j, j == 0, j == 1, True)

        with pe.Fori(0, 2) as r3:
            for c in range(3):
                if c == 0:
                    pe.wait_ge(og["res_ok"], r3 * 3 + START)
                out_half(r3 * 6, c, 2 * c)
        pe.wait_ge(og["res_ok"], 6 + START)
        for c in range(2):
            out_half(12, c, 2 * c)

        for k2 in range(KT // 2):
            b = bank[3 + k2 % 4]
            if k2 == 0:
                pe.wait_ge(og["scaled_ok"], TT)
            if k2 >= 4:
                pe.wait_ge(og["lo_ok"], k2 - 3)
            for j in range(2):
                for t in range(TT):
                    k = 2 * k2 + j
                    mi = nc.tensor.transpose(b[:, j * S + t * P:j * S + (t + 1) * P], htok[:, t, k * P:(k + 1) * P], ident[:, :])
            mi.then_inc(og["tr_ps"], 1)
        pe.wait_ge(og["lo_ok"], KT // 2)
        pe.wait_ge(og["wlo_ok"], 1)
        for k in range(KT):
            for j, xx in enumerate((xhi, xlo)):
                mi = nc.tensor.matmul(bank[7][:, 0:S], wrt_st[:, k, :], xx[:, k, :], start=k == 0 and j == 0,
                                      stop=k == KT - 1 and j == 1)
        mi.then_inc(rt["ps"], 1)
        for c in range(2):
            for j in range(2):
                n = N_S0 + 2 * c + j
                dense(pe, n, n, bank[c], xhi, xlo, UK * j, j == 0, j == 1, False)
            if c == 0:
                pe.wait_ge(rt["sum_ok"], 1)
                for t in range(TT):
                    mi = nc.tensor.matmul(bank[7][:, S + t * E:S + (t + 1) * E], rsum[:, t * P:(t + 1) * P], stack_id[:, :],
                                          start=True, stop=True)
                mi.then_inc(rt["lg_ps"], 1)
        pe.wait_ge(rt["sel_ok"], 1)
        nc.tensor.matmul(bank[7][:, 0:E], before[:, :], sel[:, 0, :], start=True, stop=True)
        nc.tensor.matmul(bank[7][:, E:2 * E], before[:, :], sel[:, 1, :], start=True, stop=False)
        nc.tensor.matmul(bank[7][:, E:2 * E], ones[:, :], sel[:, 0, :], start=False, stop=True)
        nc.tensor.matmul(bank[7][:, 2 * E:3 * E], ones[:, :], sel[:, 0, :], start=True, stop=False)
        nc.tensor.matmul(bank[7][:, 2 * E:3 * E], ones[:, :], sel[:, 1, :], start=False, stop=True).then_inc(rt["rk_ps"], 1)
        pe.wait_ge(sh["lo_ok"], 1)
        for j in range(2):
            n = N_D0 + j
            pe.wait_ge(lo_done, n + 1)
            for t in range(TT):
                for c in range(2):
                    i = 4 * j + 2 * t + c
                    b = bank[2 + i % 5]
                    if i >= 5:
                        pe.wait_ge(sh["acc_ok"], i - 4)
                    for f in range(2):
                        sl = slice(f * 1024 + c * 512, f * 1024 + (c + 1) * 512)
                        for jj, (a, w) in enumerate(((shi, whi), (slo, whi), (shi, wlo))):
                            mi = nc.tensor.matmul(b[:, :], a[:, f, t * P:(t + 1) * P], w[n % SPLIT][:, sl],
                                                  start=f == 0 and jj == 0, stop=f == 1 and jj == 2)
                    mi.then_inc(sh["dps"], 1)
        pe.wait_ge(sh["dps"], 8)
        pe.sem_inc(unit_used, 2)
        pe.wait_ge(rt["rounds_ok"], 1)
        pe.sem_inc(ex["gu_free"], 4)
        pe.wait_ge(sh["acc_ok"], 8)
        n_rounds = pe.value_load(rounds[0:1, 0:1], min_val=1, max_val=4)
        with pe.Fori(0, n_rounds) as b:
            def gather(g):
                pe.wait_ge(ex["pick_ok"], b * (PAIRS + 2) + (g + 1))
                for k4 in range(4):
                    pe.wait_ge(ex[("xg_act", "xg_dve")[k4 % 2]], b * (2 * PAIRS + 2) + (g * 2 + k4 // 2) + START)
                    for k in range(4):
                        for t in range(TT):
                            mi = nc.tensor.matmul(bank[k4 % 2][:, k * P:(k + 1) * P],
                                                  htok[:, t, (4 * k4 + k) * P:(4 * k4 + k + 1) * P],
                                                  pick[:, t, :, :].rearrange("p j s -> p (j s)"),
                                                  start=t == 0, stop=t == TT - 1)
                    mi.then_inc(ex["ga_ps"], 1)

            def scatter(i):
                for t in range(TT):
                    for c in range(4):
                        pe.wait_ge(ex["acc_ok"], b * (8 * PAIRS + 8) + i * 8 + max(0, 4 * t + c - 1) + START)
                        nc.tensor.matmul(bank[6 + c % 2][:, :], pickT[:, t, :], ye[:, c * 512:(c + 1) * 512],
                                         start=True, stop=True).then_inc(ex["sc_ps"], 1)

            pe.wait_ge(ex["zero"], b * 2 + 2)
            gather(0)
            with pe.Fori(0, PAIRS) as pair:
                it = b * PAIRS + pair
                pe.wait_ge(ex["xg_act"], b * (2 * PAIRS + 2) + (pair * 2 + 2) + START)
                pe.wait_ge(ex["xg_dve"], b * (2 * PAIRS + 2) + (pair * 2 + 2) + START)
                pe.wait_ge(ex["a_ok"], it + START)
                for c in range(4):
                    pe.wait_ge(gu_full[c], it * 32 + 32)
                    for k in range(4):
                        for j in range(2):
                            mi = nc.tensor.matmul(bank[3][CAP * j:CAP * j + CAP, :], xg[:, 4 * c + k, CAP * j:CAP * j + CAP],
                                                  wgu_t[j][:, c, k, :], start=c == 0 and k == 0, stop=c == 3 and k == 3)
                    mi.then_inc(ex["gu_free"], 1)
                gather(pair + 1)
                pe.wait_ge(ex["a_ok"], it + 1 + START)
                pe.wait_ge(ex["pt_ok"], it + START)
                for f in range(2):
                    mi = nc.tensor.transpose(bank[2][:, f * P:(f + 1) * P], eact[:, f * P:(f + 1) * P], ident[:, :])
                mi.then_inc(ex["at_ps"], 1)
                pe.wait_ge(ex["y_ok"], it * 4 + START)
                scatter(pair)
                pe.wait_ge(ex["pickw_ok"], it + 1)
                pe.wait_ge(ex["at_ok"], it + 1)
                for t in range(TT):
                    mi = nc.tensor.transpose(bank[2][:, S + t * P:S + (t + 1) * P],
                                             pickw[:, t, :, :].rearrange("p j s -> p (j s)"), ident[:, :])
                mi.then_inc(ex["pt_ps"], 1)
                for c in range(4):
                    pe.wait_ge(ex["y_ok"], it * 4 + max(0, c - 1) + START)
                    for f in range(2):
                        pe.wait_ge(d_full[f], it * 32 + 32)
                        for j in range(2):
                            mi = nc.tensor.matmul(bank[4 + c % 2][CAP * j:CAP * j + CAP, :], eactT[:, f, CAP * j:CAP * j + CAP],
                                                  wd_t[j][:, f, c * 512:(c + 1) * 512], start=f == 0, stop=f == 1)
                    mi.then_inc(ex["y_ps"], 1)
            pe.wait_ge(ex["y_ok"], b * (4 * PAIRS) + 4 * PAIRS + START)
            pe.wait_ge(ex["pt_ok"], b * PAIRS + PAIRS + START)
            scatter(PAIRS)

    @block.scalar
    def _(act):
        for n in range(N_X):
            dst = (xhi, mhi)[n // 2]
            act.wait_ge(raw_full[n % RAW], (n // RAW + 1) * 16)
            nc.scalar.activation(dst[:, UK * (n % 2):UK * (n % 2) + UK, :].rearrange("p k t -> p (k t)"),
                                 raw[n % RAW][:, :], ACT.Copy).then_inc(hi_done, 1)
        act.wait_ge(dt_in, 16)
        nc.scalar.activation(wdt_hi[:, :, :].rearrange("p k t -> p (k t)"), wdt_raw[:, :], ACT.Copy).then_inc(dt_w, 1)

        def hi(n, u, count):
            act.wait_ge(raw_full[u % RAW], count)
            act.wait_ge(unit_used, n - N_X - SPLIT + 1)
            nc.scalar.activation(whi[u % SPLIT][:, :], raw[u % RAW][:, :], ACT.Copy).then_inc(hi_done, 1)

        def hi_first(n):
            act.wait_ge(raw_full[n % RAW], (n // RAW + 1) * 16)
            nc.scalar.activation(whi[n % SPLIT][:, :], raw[n % RAW][:, :], ACT.Copy).then_inc(hi_done, 1)

        for n in (N_X, N_X + 1):
            hi_first(n)
        act.wait_ge(par_in, 64)
        nc.scalar.activation(dts[:, 7, :], aneg[:, :], ACT.Exp).then_inc(dt_a, 1)
        act.wait_ge(dt_e, 1)
        nc.scalar.activation(dts[:, 2, :], dts[:, 1, :], ACT.Exp).then_inc(dt_l, 1)
        act.wait_ge(dt_e, 2)
        nc.scalar.activation(dts[:, 4, :], dts[:, 3, :], ACT.Ln).then_inc(dt_l, 1)
        act.wait_ge(lb_e, 1)
        nc.scalar.activation(small[:, 1, :], small[:, 0, :], ACT.Exp).then_inc(lb_x, 1)
        for h in range(NH):
            if h > 0:
                for j in range(2):
                    n = N_X + 2 * h + j
                    hi(n, n, (n // RAW + 1) * 16)
            act.wait_ge(unit_used, 2 * h + 2)
            if h < 4:
                o = kT[:, 2 * h:2 * h + 2, :]
            else:
                o = vmem[:, :, (h - 4) * UC:(h - 3) * UC]
            nc.scalar.activation(o, bank[h % 3][:, :].rearrange("p (t c) -> p t c", t=2), ACT.Copy).then_inc(mem_read, 1)
        with act.Fori(0, PARTS) as p:
            def b3(b):
                return bank[b][:, :].rearrange("p (t c) -> p t c", t=2)

            for u in range(UP + 1):
                if u < UP:
                    n = N_P0 + u
                    hi(p * UP + n, n, unit_wait(p, UP, N_P0, u))
                if u == 0:
                    act.wait_ge(s["dp_ps"], p + START)
                    act.wait_ge(unit_used, 2 * NH)
                    act.dma_start(poolmix[:, :, :], poolm[p]).then_inc(s["pmix_in"], 16)
                    act.wait_ge(s["yp_ps"], p + START)
                    act.dma_start(poolwt[:, :, :], poolw[p]).then_inc(s["pw_in"], 16)
                if u == 2:
                    act.wait_ge(unit_used, half_count(p, 1))
                    act.wait_ge(s["dp_ps"], p + START)
                    nc.scalar.activation(upool[:, :, :], b3(0), ACT.Copy).then_inc(s["u_ok"], 1)
                if 2 <= u < 5:
                    b = (0, 2, 1)[u - 2]
                    act.wait_ge(s["dec_ps"], cnt(p, 3, u - 1) + START)
                    act.wait_ge(s["y_ps"], p + START)
                    nc.scalar.activation(dec[:, b, :, :], bank[5][:, :].rearrange("p (h l) -> p h l", h=4), ACT.Exp)\
                        .then_inc(s["dec_ok"], 1)
                if u == 4:
                    act.wait_ge(unit_used, half_count(p, 2))
                    act.wait_ge(s["sc_ps"], p + START)
                    nc.scalar.activation(qm[:, :, :], b3(1), ACT.Copy).then_inc(s["qm_ok"], 1)
                    act.wait_ge(s["dp_ps"], p + 1 + START)
                    act.wait_ge(s["yp_ps"], p + START)
                    nc.scalar.activation(dpool[:, :, :], b3(3), ACT.Copy).then_inc(s["dp_ok"], 1)
                if u == 6:
                    act.wait_ge(unit_used, half_count(p, 3))
                    act.wait_ge(s["kk_ok"], p + START)
                    nc.scalar.activation(fr[:, :, :], b3(2), ACT.Exp).then_inc(s["f_exp"], 1)
                    act.wait_ge(s["nmx_ok"], p + 1)
                    act.wait_ge(s["pt_ps"], p + START)
                    for t in range(TT):
                        nc.scalar.activation(prob[:, t, :], bank[3][:, t * S:(t + 1) * S], ACT.Exp,
                                             bias=small[:, 1, t:t + 1], scale=UC ** -0.5,
                                             accum_out=small[:, 2, t:t + 1]).then_inc(s["p_ok"], 1)
                if u == 8:
                    act.wait_ge(unit_used, half_count(p, 4))
                    act.wait_ge(s["oss_ps"], p + START)
                    nc.scalar.activation(th[:, :, :], b3(0), ACT.Tanh, scale=0.5).then_inc(s["qt_ok"], 1)
                if u == 10:
                    act.wait_ge(unit_used, half_count(p, 5))
                    act.wait_ge(s["cv_ok"], 2 * p + START)
                    act.wait_ge(upz, 1)
                    nc.scalar.activation(up[:, 0:2, 3:3 + S], b3(1), ACT.Copy).then_inc(s["up_ok"], 1)
                    act.wait_ge(s["pt_ps"], p + 1 + START)
                    act.wait_ge(s["cx_ps"], p + START)
                    nc.scalar.activation(probT[:, :, :], b3(4), ACT.Copy).then_inc(s["pt_ok"], 1)
                if u == 12:
                    act.wait_ge(unit_used, half_count(p, 6))
                    nc.scalar.activation(up[:, 2:4, 3:3 + S], b3(2), ACT.Copy).then_inc(s["up_ok"], 1)
                    act.wait_ge(s["cv_ok"], cnt(p, 2, 1) + START)
                    act.wait_ge(s["yss_ps"], p + START)
                    nc.scalar.activation(tc[:, 0:2, :], cv[:, 0:2, :], ACT.Tanh, scale=0.5).then_inc(s["tc_ok"], 1)
                    act.wait_ge(s["cx_ps"], p + 1 + START)
                    nc.scalar.activation(yT[:, 3, bass.ts(p, 2), :], b3(3), ACT.Copy).then_inc(s["cx_ok"], 1)
                if u == 14:
                    act.wait_ge(unit_used, half_count(p, 7))
                    act.wait_ge(s["lev_ok"], cnt(p, 17, 1))
                    nc.scalar.activation(th[:, :, :], b3(0), ACT.Tanh, scale=0.5).then_inc(s["gt_ok"], 1)
                    act.wait_ge(s["cv_ok"], cnt(p, 2, 2) + START)
                    nc.scalar.activation(tc[:, 2:4, :], cv[:, 2:4, :], ACT.Tanh, scale=0.5).then_inc(s["tc_ok"], 1)
                if u == 16:
                    act.wait_ge(unit_used, half_count(p, 8))
                    act.wait_ge(s["o_ps"], p + START)
                    nc.scalar.activation(vh[:, :, :], b3(1), ACT.Copy).then_inc(s["vh_ok"], 1)
                if u == 17:
                    act.wait_ge(s["x_ps"], p + 1 + START)
                    nc.scalar.activation(attx[:, :, :], bank[6][:, 0:2 * P].rearrange("p (h l) -> p h l", h=2), ACT.Copy)\
                        .then_inc(s["x_ok"], 1)
                if u == 18:
                    act.wait_ge(unit_used, half_count(p, 9))
                    nc.scalar.activation(zs[:, :, :], b3(2), ACT.Tanh, scale=0.5).then_inc(s["tz_ok"], 1)
                    act.wait_ge(s["o_ps"], p + 1 + START)
                    nc.scalar.activation(osq, bank[7][:, :], ACT.Square).then_inc(s["osq_ok"], 1)
                    act.wait_ge(s["y1_ok"], p + 1 + START)
                    nc.scalar.activation(tc[:, 0:2, :], yss[:, :, :], ACT.Square).then_inc(s["ysq_ok"], 1)
                    act.wait_ge(s["ovar_ok"], p + 1)
                    nc.scalar.activation(rh, rh, ACT.Sqrt).then_inc(s["osd_ok"], 1)
                    act.wait_ge(s["yvar_ok"], p + 1)
                    nc.scalar.activation(rs[:, :], rs[:, :], ACT.Sqrt).then_inc(s["ysd_ok"], 1)


        act.wait_ge(s["ys_ok"], 2 * PARTS + START)
        act.wait_ge(s["yh_ok"], PARTS + START)
        act.wait_ge(s["yp_ok"], 2 * PARTS)
        act.wait_ge(s["yss_ps"], PARTS + START)
        for n in range(4):
            nc.scalar.activation(yhi[n][:, :, :], yT[:, n, :, :], ACT.Copy).then_inc(mg["y_hi"], 1)
        with act.Fori(0, DBLK) as b:
            for u in range(UM):
                n = N_M0 + u
                hi(b * UM + n, n, unit_wait(b, UM, N_M0, u))
                if u % 3 == 2:
                    act.wait_ge(unit_used, b * UM + (n - N_X))
                    if u == 2:
                        act.wait_ge(mg["mul_ok"], b * 4 + START)
                        act.wait_ge(mg["y_lo"], 4)
                    nc.scalar.activation(sig[:, u // 3, :], bank[2 * (u // 3)][:, :], ACT.Tanh, scale=0.5)\
                        .then_inc(mg["gate_ok"], 1)
        with act.Fori(0, 2) as r:
            for u in range(6):
                hi(r * 6 + (N_O0 + u), N_O0 + u, unit_wait(r, 6, N_O0, u))
        for u in range(12, 16):
            n = N_O0 + u
            hi(n, n, (n // RAW + 1) * 16)

        def norm_part(k):
            for t in range(TT):
                act.wait_ge(og["stats_ok"], k * TT + t + 1)
                nc.scalar.activation(bnr[:, t, 1:2], bnr[:, t, 0:1], ACT.Sqrt).then_inc(og["sd_ok"], 1)
            for t in range(TT):
                v = (htok, acc)[k][:, t, :]
                act.wait_ge(og["ln_ch"], k * TT + t + 1)
                nc.scalar.activation(v, v, ACT.Identity, scale=bnr[:, t, 2:3], bias=bnr[:, t, 3:4]).then_inc(og["nrm_ok"], 1)

        act.wait_ge(og["w_in"], 32)
        nc.scalar.activation(wrt_st[:, :, 0:E], wrt_raw[:, :, :], ACT.Copy).then_inc(og["whi_ok"], 1)
        norm_part(0)
        for k2 in range(KT // 2):
            act.wait_ge(og["tr_ps"], k2 + 1)
            nc.scalar.activation(xhi[:, 2 * k2:2 * k2 + 2, :], bank[3 + k2 % 4][:, :].rearrange("p (k t) -> p k t", k=2),
                                 ACT.Copy).then_inc(og["hi_ok"], 1)
        for n in (N_S0, N_S0 + 1):
            hi(n, n, (n // RAW + 1) * 16)
        act.wait_ge(rt["ps"], 1)
        nc.scalar.activation(rsum[:, :], bank[7][:, 0:S], ACT.Copy).then_inc(rt["sum_ok"], 1)
        for n in (N_S0 + 2, N_S0 + 3):
            hi(n, n, (n // RAW + 1) * 16)
        act.wait_ge(rt["lg_ps"], 1)
        nc.scalar.activation(score[:, :, :], bank[7][:, S:S + TT * E].rearrange("p (t e) -> p t e", t=TT), ACT.Exp,
                             scale=-1.0).then_inc(rt["exp_ok"], 1)
        for n in (N_D0, N_D0 + 1):
            hi(n, n, (n // RAW + 1) * 16)
        act.wait_ge(unit_used, N_D0 - 2 - N_X)
        nc.scalar.activation(sth[:, :], bank[0][:, :], ACT.Tanh, scale=0.5).then_inc(sh["th_ok"], 1)
        act.wait_ge(sh["a_ok"], 1)
        nc.scalar.activation(shi[:, :, :], sact[:, :].rearrange("p (c t) -> p c t", c=2), ACT.Copy).then_inc(sh["hi_ok"], 1)

        act.wait_ge(rt["rounds_ok"], 1)
        n_rounds = act.value_load(rounds[0:1, 0:1], min_val=1, max_val=4)
        with act.Fori(0, n_rounds) as b:
            def gathered(g, gu):
                act.wait_ge(ex["gu_free"], gu * 4 + 4)
                for k4 in (0, 2):
                    act.wait_ge(ex["ga_ps"], b * (4 * PAIRS + 4) + (g * 4 + k4 + 1) + START)
                    nc.scalar.activation(xg[:, 4 * k4:4 * k4 + 4, :], bank[0][:, :].rearrange("p (k s) -> p k s", k=4),
                                         ACT.Copy).then_inc(ex["xg_act"], 1)

            gathered(0, b * PAIRS)
            with act.Fori(0, PAIRS) as pair:
                it = b * PAIRS + pair
                act.wait_ge(ex["gu_free"], it * 4 + 8)
                nc.scalar.activation(eth[:, :], bank[3][:, 0:FE], ACT.Tanh, scale=0.5).then_inc(ex["th_ok"], 1)
                gathered(pair + 1, it + 1)
                act.wait_ge(ex["at_ps"], it + 1 + START)
                act.wait_ge(ex["y_ps"], it * 4 + START)
                nc.scalar.activation(eactT[:, :, :], bank[2][:, 0:S].rearrange("p (f s) -> p f s", f=2), ACT.Copy)\
                    .then_inc(ex["at_ok"], 1)
                act.wait_ge(ex["pt_ps"], it + 1 + START)
                act.wait_ge(ex["sc_ps"], b * (8 * PAIRS + 8) + (pair * 8 + 8))
                nc.scalar.activation(pickT[:, :, :], bank[2][:, S:2 * S].rearrange("p (t s) -> p t s", t=TT), ACT.Copy)\
                    .then_inc(ex["pt_ok"], 1)
                for c in range(4):
                    act.wait_ge(ex["y_ps"], it * 4 + (c + 1) + START)
                    nc.scalar.activation(ye[:, c * 512:(c + 1) * 512], bank[4 + c % 2][:, :], ACT.Copy)\
                        .then_inc(ex["y_ok"], 1)
        norm_part(1)

    @block.vector
    def _(dve):
        V = nc.vector

        def lo(u, n, dst=None, src_hi=None):
            dve.wait_ge(hi_done, n + 1)
            V.tensor_tensor(wlo[u % SPLIT][:, :], raw[u % RAW][:, :], whi[u % SPLIT][:, :].bitcast(f32),
                            ALU.subtract).then_inc(lo_done, 1)

        for n in range(N_X):
            h, l = ((xhi, xlo), (mhi, mlo))[n // 2]
            sl = slice(UK * (n % 2), UK * (n % 2) + UK)
            dve.wait_ge(hi_done, n + 1)
            V.tensor_tensor(l[:, sl, :].rearrange("p k t -> p (k t)"), raw[n % RAW][:, :],
                            h[:, sl, :].rearrange("p k t -> p (k t)").bitcast(f32), ALU.subtract).then_inc(lo_done, 1)
        dve.wait_ge(dt_w, 1)
        V.tensor_tensor(wdt_lo[:, :, :].rearrange("p k t -> p (k t)"), wdt_raw[:, :],
                        wdt_hi[:, :, :].rearrange("p k t -> p (k t)").bitcast(f32), ALU.subtract).then_inc(dt_w, 1)
        lo(N_X, N_X)
        lo(N_X + 1, N_X + 1)

        chain = [0]

        def link(ins):
            chain[0] += 1
            ins.then_inc(dt_chain, 1)
            dve.wait_ge(dt_chain, chain[0])

        dve.wait_ge(const_ok, N_CONST)
        link(V.tensor_tensor(xi[:, 0:P], xi[:, 0:P], xi[:, P:2 * P], ALU.bitwise_xor))
        link(V.tensor_copy(xf[:, 0, :], xi[:, 0:P]))
        link(V.tensor_tensor(xf[:, 0, :], xf[:, 0, :], before[:, :], ALU.mult))
        link(V.tensor_scalar(xf[:, 1, :], xf[:, 0, :], 1.0, None, ALU.is_ge))
        for k in range(LEVELS - 2):
            a, b = xf[:, 1 + k % 2, :], xf[:, 1 + (k + 1) % 2, :]
            link(V.tensor_scalar(b, xf[:, 0, :], float(2 ** (k + 1)), None, ALU.is_ge))
            link(V.tensor_tensor(lmask[:, k, :], a, b, ALU.subtract))
        dve.wait_ge(par_in, 64)
        dve.wait_ge(dt_ps, 1)
        v, ab, e1, u1, ln1, w1, m1, aa = (dts[:, j, :] for j in range(8))
        link(V.tensor_tensor(v, bank[7][:, 0:32], dtbias[:, :], ALU.add))
        link(V.tensor_scalar(ab, v, -1.0, None, ALU.mult))
        ins = V.tensor_tensor(ab, v, ab, ALU.min)
        ins.then_inc(dt_e, 1)
        dve.wait_ge(dt_l, 1)
        ins = V.tensor_scalar(u1, e1, 1.0, None, ALU.add)
        ins.then_inc(dt_e, 1)
        dve.wait_ge(dt_e, 2)
        link(V.tensor_scalar(w1, u1, 1.0, None, ALU.subtract))
        link(V.tensor_scalar(m1, w1, 0.0, None, ALU.is_equal))
        link(V.tensor_tensor(w1, w1, m1, ALU.add))
        link(V.reciprocal(w1, w1))
        link(V.tensor_tensor(w1, w1, e1, ALU.mult))
        dve.wait_ge(dt_l, 2)
        link(V.tensor_tensor(w1, w1, ln1, ALU.mult))
        link(V.tensor_tensor(m1, m1, e1, ALU.mult))
        link(V.tensor_tensor(w1, w1, m1, ALU.add))
        link(V.tensor_scalar(v, v, 0.0, None, ALU.max))
        link(V.tensor_tensor(v, v, w1, ALU.add))
        lbs, t0, t1 = par[:, :, 24:26], small[:, 0, :].rearrange("p (a b) -> p a b", b=2), \
            small[:, 1, :].rearrange("p (a b) -> p a b", b=2)
        V.tensor_tensor(t0, lbs, lbs, ALU.subtract).then_inc(lb_e, 1)
        dve.wait_ge(lb_x, 1)
        link(V.reciprocal(t0, t1))
        link(V.tensor_tensor(t0, t0, t1, ALU.mult))
        link(V.tensor_tensor(t1, t0, t0, ALU.subtract))
        link(V.tensor_scalar(lbs, t1, -1.0, 1.0, ALU.mult, ALU.add))
        link(V.tensor_scalar(par[:, :, 26:28], par[:, :, 26:28], 0.5, None, ALU.mult))
        dve.wait_ge(dt_a, 1)
        link(V.tensor_scalar(hdt[:, :, :].rearrange("p t h -> p (t h)"), v, 0.5, None, ALU.mult))
        link(V.tensor_tensor(v, v, aa, ALU.mult))
        link(V.tensor_scalar(ad[:, :, :].rearrange("p t h -> p (t h)"), v, -1.0, None, ALU.mult))
        for n in range(N_X + 2, N_P0):
            lo(n, n)
        dve.wait_ge(unit_used, 2 * NH)
        link(V.memset(up[:, :, 0:3], 0.0))
        V.memset(small[:, :, :], 0.0).then_inc(upz, 1)
        dve.wait_ge(upz, 1)
        with dve.Fori(0, PARTS) as p:
            c = [0]

            def step(ins):
                c[0] += 1
                ins.then_inc(s["vch"], 1)
                dve.wait_ge(s["vch"], cnt(p, VC, c[0]))

            def b3(b):
                return bank[b][:, :].rearrange("p (t c) -> p t c", t=2)

            def par_of(j):
                return prm[:, j:j + 1]

            def conv(i):
                step(V.tensor_scalar(cv[:, i, :], up[:, i, 3:3 + S], par_of(4 * i + 3), par_of(16 + i), ALU.mult, ALU.add))
                for j in range(2, -1, -1):
                    ins = V.scalar_tensor_tensor(cv[:, i, :], up[:, i, j:j + S], par_of(4 * i + j), cv[:, i, :],
                                                 ALU.mult, ALU.add)
                    if j > 0 or i % 2 == 0:
                        step(ins)
                    else:
                        ins.then_inc(s["cv_ok"], 1)
                        dve.wait_ge(s["cv_ok"], cnt(p, 2, 1 + i // 2) + START)

            def lev_step(ins, k):
                ins.then_inc(s["lev_ok"], 1)
                dve.wait_ge(s["lev_ok"], cnt(p, 17, k))

            def level_out(l):
                if l == 0:
                    dve.wait_ge(s["o_ps"], p + START)
                dve.wait_ge(s["lev_ps"], cnt(p, LEVELS - 1, l + 1))
                scores = bank[6][:, :].rearrange("p (b t) -> p b t", t=P)
                if l == 0:
                    lev_step(V.tensor_tensor(att[:, :, :], scores, ident[:, :].unsqueeze(1).broadcast_to([P, 2 * TT, P]),
                                             ALU.mult), 2)
                    lev_step(V.tensor_tensor(flat(qq), flat(qq), fgate[:, :], ALU.mult), 3)
                    return
                m = 2 ** (l - 1)
                nb = 2 * S // (2 * m)
                t = blk[l - 1][:, :].rearrange("p (b o) -> p b o", o=2)
                kv = flat(kk).rearrange("p (b m) -> p b m", m=2 * m)
                qv = flat(qq).rearrange("p (b m) -> p b m", m=2 * m)
                V.tensor_tensor(kv[:, :, 0:m], kv[:, :, 0:m], t[:, :, 1:2].broadcast_to([P, nb, m]), ALU.mult)\
                    .then_inc(s["lev_k"], 1)
                V.copy_predicated(att[:, :, :], lmask[:, l - 1:l, :].broadcast_to([P, 2 * TT, P]), scores)\
                    .then_inc(s["lev_ok"], 1)
                V.tensor_tensor(qv[:, :, m:2 * m], qv[:, :, m:2 * m], t[:, :, 0:1].broadcast_to([P, nb, m]), ALU.mult)\
                    .then_inc(s["lev_ok"], 1)
                if l < LEVELS - 2:
                    step(V.tensor_tensor(blk[l][:, :].rearrange("p (b o) -> p b o", o=1), t[:, :, 0:1], t[:, :, 1:2],
                                         ALU.mult))
                dve.wait_ge(s["lev_ok"], cnt(p, 17, 2 * l + 3))

            def flat(t):
                return t[:, :, :].rearrange("p a b -> p (a b)")

            for u in range(UP + 1):
                if u < UP:
                    lo(N_P0 + u, p * UP + (N_P0 + u))
                if u == 0:
                    dve.wait_ge(s["ys_ok"], 2 * p + START)
                    step(V.tensor_copy(prm[:, :], par[:, p, :]))
                    dve.wait_ge(s["dec_ps"], 3 * p + START)
                    for b, t, msk in ((0, 0, True), (2, 0, False), (1, 1, True)):
                        a_b = ad[:, t:t + 1, bass.ts(p, 4)].rearrange("p o h -> p h o").broadcast_to([P, 4, P])
                        if msk:
                            ins = V.tensor_tensor(ta[:, b, :, :], a_b, upto[:, :].unsqueeze(1).broadcast_to([P, 4, P]),
                                                  ALU.mult)
                        else:
                            ins = V.tensor_copy(ta[:, b, :, :], a_b)
                        ins.then_inc(s["ta_ok"], 1)
                if u == 6:
                    dve.wait_ge(s["sc_ps"], p + 1 + START)
                    step(V.tensor_reduce(small[:, 0, 0:2], b3(3), AX.X, ALU.max))
                    dve.wait_ge(s["p_ok"], 2 * p + START)
                    V.tensor_scalar(small[:, 1, 0:2], small[:, 0, 0:2], -(UC ** -0.5), None, ALU.mult)\
                        .then_inc(s["nmx_ok"], 1)
                    dve.wait_ge(s["yp_ps"], p + 1 + START)
                    for j in range(2):
                        V.tensor_scalar(yT[:, 0, p * 2 + j, :], bank[4][:, j * S:(j + 1) * S], par_of(20 + j), None,
                                        ALU.mult).then_inc(s["yp_ok"], 1)
                if u == 7:
                    dve.wait_ge(s["f_exp"], p + 1)
                    step(V.tensor_scalar(fr[:, :, :], fr[:, :, :], 1.0, None, ALU.add))
                    step(V.reciprocal(fr[:, :, :], fr[:, :, :]))
                    for h in range(2):
                        step(V.tensor_scalar(fr[:, h, :], fr[:, h, :], par_of(24 + h), None, ALU.mult))
                    step(V.tensor_scalar(fgate[:, :], flat(fr), -1.0, 1.0, ALU.mult, ALU.add))
                    dve.wait_ge(s["x_ps"], p + START)
                    V.tensor_scalar(flat(kk), flat(fr), 0.5, None, ALU.mult).then_inc(s["kk_ok"], 1)
                    dve.wait_ge(s["kk_ok"], p + 1 + START)
                if u == 8:
                    dve.wait_ge(s["p_ok"], 2 * p + 2 + START)
                    step(V.reciprocal(small[:, 3, 0:2], small[:, 2, 0:2]))
                    step(V.tensor_scalar(prob[:, 0, :], prob[:, 0, :], small[:, 3, 0:1], None, ALU.mult))
                    V.tensor_scalar(prob[:, 1, :], prob[:, 1, :], small[:, 3, 1:2], None, ALU.mult).then_inc(s["pn_ok"], 1)
                    dve.wait_ge(s["qt_ok"], p + 1)
                    lev_step(V.scalar_tensor_tensor(qq[:, :, :], th[:, :, :], 1.0, b3(0), ALU.add, ALU.mult), 1)
                if 9 <= u < 17:
                    level_out(u - 9)
                if u == 11:
                    dve.wait_ge(s["up_ok"], cnt(p, 2, 1))
                    conv(0)
                if u == 12:
                    conv(1)
                if u == 13:
                    dve.wait_ge(s["up_ok"], cnt(p, 2, 2))
                    conv(2)
                    dve.wait_ge(s["tc_ok"], cnt(p, 2, 1))
                    V.scalar_tensor_tensor(cv[:, 0:2, :], tc[:, 0:2, :], 1.0, cv[:, 0:2, :], ALU.add, ALU.mult)\
                        .then_inc(s["xc_ok"], 1)
                if u == 14:
                    conv(3)
                if u == 15:
                    dve.wait_ge(s["tc_ok"], cnt(p, 2, 2))
                    V.scalar_tensor_tensor(cv[:, 2:4, :], tc[:, 2:4, :], 1.0, cv[:, 2:4, :], ALU.add, ALU.mult)\
                        .then_inc(s["xc_ok"], 1)
                    dve.wait_ge(s["gt_ok"], p + 1)
                    V.scalar_tensor_tensor(gs[:, :, :], th[:, :, :], 1.0, b3(0), ALU.add, ALU.mult).then_inc(s["gs_ok"], 1)
                if u == 16:
                    dve.wait_ge(s["xtp_ps"], p + 1)
                    for t in range(TT):
                        V.tensor_tensor(xt[:, t, :].rearrange("p (h c) -> p h c", h=4),
                                        bank[4][:, t * UC:(t + 1) * UC].rearrange("p (h c) -> p h c", h=4),
                                        hdt[:, t:t + 1, bass.ts(p, 4)].rearrange("p o h -> p h o").broadcast_to([P, 4, 64]),
                                        ALU.mult).then_inc(s["xt_ok"], 1)
                if u == 17:
                    dve.wait_ge(s["cb_ps"], p + 1)
                    V.tensor_tensor(cbm[:, :, :], bank[3][:, 0:3 * P].rearrange("p (b l) -> p b l", b=3), quart[:, :, :],
                                    ALU.mult).then_inc(s["cb_ok"], 1)
                    dve.wait_ge(s["cb_ok"], p + 1)
                    dve.wait_ge(s["dec_ok"], 3 * p + 3)
                    V.tensor_tensor(dec[:, :, :, :], dec[:, :, :, :],
                                    cbm[:, :, :].unsqueeze(2).broadcast_to([P, 3, 4, P]), ALU.mult).then_inc(s["g_ok"], 1)
                if u == 18:
                    dve.wait_ge(s["y_ps"], p + 1 + START)
                    for j in range(2):
                        step(V.scalar_tensor_tensor(yss[:, j, :], cv[:, j, :], par_of(26 + j), bank[5][:, j * S:(j + 1) * S],
                                                    ALU.mult, ALU.add))
                    dve.wait_ge(s["tz_ok"], p + 1)
                    step(V.scalar_tensor_tensor(zs[:, :, :], zs[:, :, :], 1.0, b3(2), ALU.add, ALU.mult))
                    V.scalar_tensor_tensor(yss[:, :, :], yss[:, :, :], 0.5, zs[:, :, :], ALU.mult, ALU.mult)\
                        .then_inc(s["y1_ok"], 1)
                    dve.wait_ge(s["oss_ps"], p + 1 + START)
                    V.tensor_scalar(rh, bank[3][:, :], 1.0 / P, EPS, ALU.mult, ALU.add).then_inc(s["ovar_ok"], 1)
                    dve.wait_ge(s["yss_ps"], p + 1 + START)
                    V.tensor_scalar(rs[:, :], bank[4][:, 0:S], 1.0 / UC, EPS, ALU.mult, ALU.add).then_inc(s["yvar_ok"], 1)
                    dve.wait_ge(s["osd_ok"], p + 1)
                    step(V.reciprocal(rh, rh))
                    step(V.scalar_tensor_tensor(rh, bank[7][:, :], hnw[:, 0:1], rh, ALU.mult, ALU.mult))
                    V.scalar_tensor_tensor(yT[:, 2, bass.ts(p, 2), :], rh.rearrange("p (a b) -> p a b", a=2), 0.5,
                                           gs[:, :, :], ALU.mult, ALU.mult).then_inc(s["yh_ok"], 1)
                    dve.wait_ge(s["ysd_ok"], p + 1)
                    step(V.reciprocal(rs[:, :], rs[:, :]))
                    for j in range(2):
                        V.scalar_tensor_tensor(yT[:, 1, p * 2 + j, :], yss[:, j, :], par_of(22 + j), rs[:, :],
                                               ALU.mult, ALU.mult).then_inc(s["ys_ok"], 1)
            assert c[0] == VC, c[0]


        dve.wait_ge(s["ys_ok"], 2 * PARTS + START)
        dve.wait_ge(s["cx_ok"], PARTS)
        for n in range(4):
            dve.wait_ge(mg["y_hi"], n + 1)
            V.tensor_tensor(ylo[n][:, :, :], yT[:, n, :, :], yhi[n][:, :, :].bitcast(f32), ALU.subtract).then_inc(mg["y_lo"], 1)
        dve.wait_ge(mg["y_lo"], 4)
        with dve.Fori(0, DBLK) as b:
            c = [0]

            def mstep(ins):
                c[0] += 1
                ins.then_inc(mg["ch"], 1)
                dve.wait_ge(mg["ch"], b * 5 + c[0])

            for u in range(UM + 1):
                if u < UM:
                    lo(N_M0 + u, b * UM + (N_M0 + u))
                if u % 3 == 0 and u > 0:
                    n = u // 3 - 1
                    dve.wait_ge(mg["gate_ok"], b * 4 + (n + 1) + START)
                    dve.wait_ge(unit_used, b * UM + (N_M0 + u - N_X))
                    if n == 0:
                        dve.wait_ge(mg["block_ok"], b + START)
                    dst = macc if n == 0 else mtmp
                    V.scalar_tensor_tensor(dst[:, :], sig[:, n, :], 1.0, bank[2 * n + 1][:, :], ALU.add, ALU.mult)\
                        .then_inc(mg["mul_ok"], 1)
                    dve.wait_ge(mg["mul_ok"], b * 4 + (n + 1) + START)
                    if n > 0:
                        mstep(V.tensor_tensor(macc[:, :], macc[:, :], mtmp[:, :], ALU.add))
            acc3 = macc[:, :].rearrange("p (c t) -> p c t", c=2)
            gh, gl = ghi[:, bass.ts(b, 2), :], glo[:, bass.ts(b, 2), :]
            mstep(V.tensor_scalar(gh, acc3, 0.5, None, ALU.mult))
            mstep(V.tensor_scalar(macc[:, :], macc[:, :], 0.5, None, ALU.mult))
            V.tensor_tensor(gl, acc3, gh.bitcast(f32), ALU.subtract).then_inc(mg["block_ok"], 1)
            assert c[0] == 5

        def residual(cnt_used, cols, k):
            dve.wait_ge(unit_used, cnt_used)
            hs = htok[:, :, cols]
            V.scalar_tensor_tensor(hs, hs, ALPHA, bank[k % 3][:, :].rearrange("p (t c) -> p t c", t=TT), ALU.mult,
                                   ALU.add).then_inc(og["res_ok"], 1)

        with dve.Fori(0, 2) as r:
            for u in range(7):
                if u < 6:
                    lo(N_O0 + u, r * 6 + (N_O0 + u))
                if u % 2 == 0 and u > 0:
                    if u == 2:
                        dve.wait_ge(og["x_in"], 16 * TT)
                    residual(r * 6 + (N_O0 + u - N_X), bass.ds(r * (3 * UC) + (u // 2 - 1) * UC, UC), u // 2 - 1)
        for u in range(12, 17):
            n = N_O0 + u
            if u < 16:
                lo(n, n)
            if u % 2 == 0 and u > 12:
                residual(n - N_X, slice((u // 2 - 1) * UC, u // 2 * UC), u // 2 - 1)

        lch = [0]

        def lstep(ins):
            lch[0] += 1
            ins.then_inc(rt["ch"], 1)
            dve.wait_ge(rt["ch"], lch[0])

        def norm_stats(k):
            src = (htok, acc)[k]
            if k == 0:
                dve.wait_ge(og["res_ok"], DBLK + START)
            for t in range(TT):
                for c in range(4):
                    lstep(V.bn_stats(bns[:, t, c, :], src[:, t, c * 512:(c + 1) * 512]))
                lstep(V.bn_aggr(bna[:, t, :], bns[:, t, :, :]))
                V.tensor_scalar(bnr[:, t, 0:1], bna[:, t, 1:2], EPS, None, ALU.add).then_inc(og["stats_ok"], 1)
            for t in range(TT):
                dve.wait_ge(og["sd_ok"], k * TT + t + 1)
                lstep(V.reciprocal(bnr[:, t, 2:3], bnr[:, t, 1:2]))
                V.scalar_tensor_tensor(bnr[:, t, 3:4], bna[:, t, 0:1], -1.0, bnr[:, t, 2:3], ALU.mult, ALU.mult)\
                    .then_inc(og["ln_ch"], 1)

        def norm_scale(k):
            src = (htok, acc)[k]
            for t in range(TT):
                dve.wait_ge(og["nrm_ok"], k * TT + t + 1)
                lstep(V.tensor_tensor(src[:, t, :], src[:, t, :], lng[k][:, :], ALU.mult))
                V.tensor_tensor(src[:, t, :], src[:, t, :], lnb[k][:, :], ALU.add).then_inc(og["scaled_ok"], 1)

        norm_stats(0)
        dve.wait_ge(og["whi_ok"], 1)
        V.tensor_tensor(wrt_st[:, :, E:2 * E], wrt_raw[:, :, :], wrt_st[:, :, 0:E].bitcast(f32), ALU.subtract)\
            .then_inc(og["wlo_ok"], 1)
        lstep(V.tensor_tensor(stack_id[:, :], ident[:, 0:E], ident[:, E:2 * E], ALU.add))
        dve.wait_ge(og["ln_in"], 32)
        norm_scale(0)
        for k2 in range(KT // 2):
            dve.wait_ge(og["hi_ok"], k2 + 1)
            sl = slice(2 * k2, 2 * k2 + 2)
            V.tensor_tensor(xlo[:, sl, :], bank[3 + k2 % 4][:, :].rearrange("p (k t) -> p k t", k=2),
                            xhi[:, sl, :].bitcast(f32), ALU.subtract).then_inc(og["lo_ok"], 1)
        for n in (N_S0, N_S0 + 1):
            lo(n, n)
        dve.wait_ge(og["scaled_ok"], TT)
        lstep(V.tensor_scalar(acc[:, :, :], htok[:, :, :], ALPHA, None, ALU.mult))
        for n in (N_S0 + 2, N_S0 + 3):
            lo(n, n)
        dve.wait_ge(og["w_in"], 32)
        dve.wait_ge(rt["exp_ok"], 1)
        lstep(V.tensor_scalar(score[:, :, :], score[:, :, :], 1.0, None, ALU.add))
        lstep(V.reciprocal(score[:, :, :], score[:, :, :]))
        lstep(V.tensor_tensor(choice[:, :, :], score[:, :, :], rbias_t[:, :].unsqueeze(1).broadcast_to(EE), ALU.add))
        for n in (N_D0,):
            lo(n, n)
        for t in range(TT):
            for g in range(GROUPS):
                lstep(V.max(gmax[:, t, g, :], choice[:, t, g * 8:(g + 1) * 8]))
        lstep(V.tensor_tensor(gsum[:, :, :], gmax[:, :, :, 0], gmax[:, :, :, 1], ALU.add))
        ga = gsum[:, :, :].unsqueeze(2).broadcast_to([P, TT, GROUPS, GROUPS])
        gb = gsum[:, :, :].unsqueeze(3).broadcast_to([P, TT, GROUPS, GROUPS])
        lstep(V.tensor_tensor(gcmp[:, :, :, :], ga, gb, ALU.is_equal))
        lstep(V.tensor_tensor(gcmp[:, :, :, :], gcmp[:, :, :, :],
                              glt[:, :, :].unsqueeze(1).broadcast_to([P, TT, GROUPS, GROUPS]), ALU.mult))
        lstep(V.tensor_tensor(gcmp2[:, :, :, :], ga, gb, ALU.is_gt))
        lstep(V.tensor_tensor(gcmp[:, :, :, :], gcmp[:, :, :, :], gcmp2[:, :, :, :], ALU.add))
        lstep(V.tensor_reduce(gpen[:, :, :], gcmp[:, :, :, :], AX.X, ALU.add))
        lstep(V.tensor_scalar(gmask[:, :, :], gpen[:, :, :], float(TOPG), None, ALU.is_lt))
        lstep(V.tensor_scalar(gpen[:, :, :], gmask[:, :, :], 1.0, -MASK_SCORE, ALU.subtract, ALU.mult))
        shape8 = [P, TT, GROUPS, E // GROUPS]
        v8 = lambda a: a[:, :, :].rearrange("p t (g e) -> p t g e", g=GROUPS)
        lstep(V.tensor_tensor(v8(masked), v8(choice), gmask[:, :, :].unsqueeze(3).broadcast_to(shape8), ALU.mult))
        lstep(V.tensor_tensor(v8(masked), v8(masked), gpen[:, :, :].unsqueeze(3).broadcast_to(shape8), ALU.add))
        lo(N_D0 + 1, N_D0 + 1)
        for t in range(TT):
            lstep(V.max(top8[:, t, :], masked[:, t, :]))
            lstep(V.match_replace(repl[:, t, :], top8[:, t, :], masked[:, t, :], -3e38))
        V.tensor_tensor(sel[:, :, :], masked[:, :, :], repl[:, :, :], ALU.not_equal).then_inc(rt["sel_ok"], 1)
        dve.wait_ge(sh["th_ok"], 1)
        lstep(V.scalar_tensor_tensor(sact[:, :], sth[:, :], 1.0, bank[0][:, :], ALU.add, ALU.mult))
        dve.wait_ge(unit_used, N_D0 - N_X)
        V.scalar_tensor_tensor(sact[:, :], sact[:, :], 0.5, bank[1][:, :], ALU.mult, ALU.mult).then_inc(sh["a_ok"], 1)
        dve.wait_ge(sh["hi_ok"], 1)
        V.tensor_tensor(slo[:, :, :], sact[:, :].rearrange("p (c t) -> p c t", c=2), shi[:, :, :].bitcast(f32),
                        ALU.subtract).then_inc(sh["lo_ok"], 1)
        dve.wait_ge(rt["sel_ok"], 1)
        lstep(V.tensor_tensor(wsel[:, :, :], score[:, :, :], sel[:, :, :], ALU.mult))
        lstep(V.tensor_reduce(wsum[:, :, 0:1], wsel[:, :, :], AX.X, ALU.add))
        lstep(V.reciprocal(wsum[:, :, 1:2], wsum[:, :, 0:1]))
        lstep(V.memset(rank[:, :, :], -1000.0))
        lstep(V.memset(wgt[:, :, :], 0.0))
        for t in range(TT):
            lstep(V.tensor_scalar(wgt[:, t, 0:E], wsel[:, t, :], wsum[:, t, 1:2], ROUTED_SCALE, ALU.mult, ALU.mult))
        dve.wait_ge(rt["rk_ps"], 1)
        lstep(V.tensor_scalar(rtmp[:, :, :], bank[7][:, 0:2 * E].rearrange("p (t e) -> p t e", t=TT), 1000.0, None, ALU.add))
        lstep(V.tensor_tensor(rtmp[:, :, :], rtmp[:, :, :], sel[:, :, :], ALU.mult))
        lstep(V.tensor_scalar(rank[:, :, 0:E], rtmp[:, :, :], 1000.0, None, ALU.subtract))
        lstep(V.tensor_reduce(rcnt[:, 0:1], bank[7][:, 2 * E:3 * E], AX.X, ALU.max))
        lstep(V.tensor_scalar(rcnt[:, 1:2], rcnt[:, 0:1], float(CAP), None, ALU.is_gt))
        lstep(V.tensor_scalar(rcnt[:, 2:3], rcnt[:, 0:1], float(2 * CAP), rcnt[:, 1:2], ALU.is_gt, ALU.add))
        lstep(V.tensor_scalar(rcnt[:, 3:4], rcnt[:, 0:1], float(3 * CAP), rcnt[:, 2:3], ALU.is_gt, ALU.add))
        V.tensor_scalar(rounds[:, 0:1], rcnt[:, 3:4], 1.0, None, ALU.add).then_inc(rt["rounds_ok"], 1)
        for i in range(8):
            j, t, cc = i // 4, i // 2 % 2, i % 2
            dve.wait_ge(sh["dps"], i + 1)
            a = acc[:, t, j * 1024 + cc * 512:j * 1024 + (cc + 1) * 512]
            V.tensor_tensor(a, a, bank[2 + i % 5][:, :], ALU.add).then_inc(sh["acc_ok"], 1)
        dve.wait_ge(sh["acc_ok"], 8)
        dve.wait_ge(rt["rounds_ok"], 1)
        dve.wait_ge(unit_used, N_UNITS - N_X)
        n_rounds = dve.value_load(rounds[0:1, 0:1], min_val=1, max_val=4)
        with dve.Fori(0, n_rounds) as b:
            PK = PAIRS + 2

            def choose(g):
                r = rank[:, :, bass.ds(g * 2, 2)].unsqueeze(3).broadcast_to([P, TT, 2, CAP])
                sl = slots[:, :].unsqueeze(1).unsqueeze(1).broadcast_to([P, TT, 2, CAP])
                V.tensor_tensor(pick[:, :, :, :], sl, r, ALU.is_equal).then_inc(ex["pick_ok"], 1)

            def gathered(g, used):
                dve.wait_ge(ex["gu_free"], used * 4 + 4)
                for k4 in (1, 3):
                    dve.wait_ge(ex["ga_ps"], b * (4 * PAIRS + 4) + (g * 4 + k4 + 1) + START)
                    V.tensor_copy(xg[:, 4 * k4:4 * k4 + 4, :], bank[1][:, :].rearrange("p (k s) -> p k s", k=4))\
                        .then_inc(ex["xg_dve"], 1)

            def add_out(i):
                for t in range(TT):
                    for c in range(4):
                        dve.wait_ge(ex["sc_ps"], b * (8 * PAIRS + 8) + (i * 8 + 4 * t + c + 1))
                        a = acc[:, t, c * 512:(c + 1) * 512]
                        V.tensor_tensor(a, a, bank[6 + c % 2][:, :], ALU.add).then_inc(ex["acc_ok"], 1)

            V.memset(ye[:, :], 0.0).then_inc(ex["zero"], 1)
            V.memset(pickT[:, :, :], 0.0).then_inc(ex["zero"], 1)
            dve.wait_ge(ex["ga_ps"], b * (4 * PAIRS + 4) + START)
            choose(0)
            gathered(0, b * PAIRS)
            choose(1)
            with dve.Fori(0, PAIRS) as pair:
                it = b * PAIRS + pair
                dve.wait_ge(ex["th_ok"], it + 1)
                dve.wait_ge(ex["at_ps"], it + START)
                V.scalar_tensor_tensor(eact[:, :], eth[:, :], 1.0, bank[3][:, 0:FE], ALU.add, ALU.mult).then_inc(ex["ch"], 1)
                dve.wait_ge(ex["ch"], it + 1)
                V.scalar_tensor_tensor(eact[:, :], eact[:, :], 0.5, bank[3][:, FE:2 * FE], ALU.mult, ALU.mult)\
                    .then_inc(ex["a_ok"], 1)
                dve.wait_ge(ex["pt_ps"], it + START)
                r = rank[:, :, bass.ds(pair * 2, 2)].unsqueeze(3).broadcast_to([P, TT, 2, CAP])
                sl = slots[:, :].unsqueeze(1).unsqueeze(1).broadcast_to([P, TT, 2, CAP])
                V.tensor_tensor(pickw[:, :, :, :], sl, r, ALU.is_equal).then_inc(ex["round_end"], 1)
                dve.wait_ge(ex["round_end"], b * (PAIRS + 1) + (pair + 1))
                V.tensor_tensor(pickw[:, :, :, :], pickw[:, :, :, :],
                                wgt[:, :, bass.ds(pair * 2, 2)].unsqueeze(3).broadcast_to([P, TT, 2, CAP]), ALU.mult)\
                    .then_inc(ex["pickw_ok"], 1)
                gathered(pair + 1, it + 1)
                choose(pair + 2)
                dve.wait_ge(ex["acc_ok"], b * (8 * PAIRS + 8) + pair * 8 + START)
                add_out(pair)
            dve.wait_ge(ex["acc_ok"], b * (8 * PAIRS + 8) + 8 * PAIRS + START)
            add_out(PAIRS)
            dve.wait_ge(ex["pick_ok"], b * PK + PK)
            dve.wait_ge(ex["pickw_ok"], b * PAIRS + PAIRS)
            dve.wait_ge(ex["sc_ps"], b * (8 * PAIRS + 8) + (8 * PAIRS + 8))
            V.tensor_scalar(rank[:, :, :], rank[:, :, :], float(CAP), None, ALU.subtract).then_inc(ex["round_end"], 1)
            dve.wait_ge(ex["round_end"], b * (PAIRS + 1) + (PAIRS + 1))
            dve.wait_ge(ex["acc_ok"], b * (8 * PAIRS + 8) + (8 * PAIRS + 8) + START)
        dve.wait_ge(ex["g2"], 32)
        norm_stats(1)
        norm_scale(1)

    blkctx.__exit__(None, None, None)


def _unit(w):
    return w.reshape(UK, P, UC).transpose(1, 0, 2).reshape(P, UK * UC)


def _columns(w):
    return [_unit(w[k:k + UK * P]) for k in range(0, w.shape[0], UK * P)]


def kernel(**inputs):
    import numpy as np
    import concourse.bacc as bacc
    from concourse.bass_utils import run_bass_kernel_spmd

    v = {k: np.asarray(a) for k, a in inputs.items()}
    w_in, w_branch = v["w_in"][0], v["w_branch"][0]
    W = PARTS * UC
    o_pool, o_z, o_xbc = 0, W, 2 * W
    o_dt = 4 * W
    o_q, o_f, o_i, o_g, o_mem, o_gate = (o_dt + 16 + W * j for j in range(6))
    units = _columns(v["x"][0].T) + _columns(v["mem"][0].T)
    for c in range(2 * PARTS):
        units += _columns(v["w_mem_kv"][0][:, c * UC:(c + 1) * UC])
    for p in range(PARTS):
        for o in (o_pool, o_mem, o_f, o_q, o_xbc):
            units += _columns(w_in[:, o + p * UC:o + (p + 1) * UC])
        o_b, o_c = o_xbc + W + p * P, o_xbc + W + W // 2 + p * P
        units += _columns(np.concatenate([w_in[:, o_b:o_b + P], w_in[:, o_c:o_c + P]], axis=1))
        for o in (o_g, o_i, o_z):
            units += _columns(w_in[:, o + p * UC:o + (p + 1) * UC])
    for b in range(DBLK):
        for n in range(4):
            units += _columns(w_in[:, o_gate + n * D + b * UC:o_gate + n * D + (b + 1) * UC])
            units += _columns(w_branch[n][:, b * UC:(b + 1) * UC])
    for b in range(DBLK):
        units += _columns(v["w_o"][0][:, b * UC:(b + 1) * UC])
    units += _columns(v["w_sh_gate"][0]) + _columns(v["w_sh_up"][0])
    for c in range(2):
        w = v["w_sh_down"][0][:, c * 1024:(c + 1) * 1024]
        units.append(w.reshape(2, P, 1024).transpose(1, 0, 2).reshape(P, UK * UC))

    params = np.zeros((P, PARTS, NP), np.float32)
    for p in range(PARTS):
        for t, c in enumerate((p * UC, p * UC + P, W + p * P, W + W // 2 + p * P)):
            params[:, p, 4 * t:4 * t + 4] = v["conv_w"][0][:, c:c + P].T
            params[:, p, 16 + t] = v["conv_b"][0][c:c + P]
        for j in range(2):
            c = p * UC + j * P
            params[:, p, 20 + j] = v["pool_scale"][0][c:c + P]
            params[:, p, 22 + j] = v["ssd_norm"][0][c:c + P]
            params[:, p, 24 + j] = v["hgrn_lb"][0][c:c + P]
            params[:, p, 26 + j] = np.repeat(v["d_skip"][0][4 * p + 2 * j:4 * p + 2 * j + 2], 64)
    pool = np.zeros((PARTS, S, S), np.float32)
    for g in range(PARTS):
        for t in range(S):
            first = max(t + 1 - 2 ** (g + 1), 0)
            pool[g, first:t + 1, t] = 1.0 / (t + 1 - first)
            pool[g, t, t] -= 1.0

    def tiles(w):
        return w.reshape(-1, P, w.shape[-1]).transpose(1, 0, 2)

    gate_up = np.concatenate([v["w_exp_gate"][0], v["w_exp_up"][0]], axis=2)
    arrays = {
        "units": np.stack(units),
        "params": params,
        "hnorm": v["hgrn_norm"][0][:, None],
        "wdt": tiles(w_in[:, o_dt:o_dt + 16]).reshape(P, KT * 16),
        "dtb": np.broadcast_to(np.tile(v["dt_bias"][0], TT), (P, TT * 16)),
        "alog": np.broadcast_to(np.tile(v["a_log"][0], TT), (P, TT * 16)),
        "poolm": pool.reshape(PARTS, TT, P, S).transpose(0, 2, 1, 3),
        "poolw": v["pool_w"][0].reshape(PARTS, 2, P, UC).transpose(0, 2, 1, 3),
        "xtok": v["x"][0],
        "lnp": np.stack([v["ln1_g"][0], v["ln1_b"][0], v["ln2_g"][0], v["ln2_b"][0]]),
        "wrt": tiles(v["w_router"][0]),
        "rbias": v["router_bias"][0],
        "wgu": gate_up.reshape(E, 4, 4, P, 2 * FE).transpose(0, 1, 3, 2, 4),
        "wd": v["w_exp_down"][0].reshape(E, 2, P, D),
    }
    arrays = {k: np.ascontiguousarray(a) for k, a in arrays.items()}
    nc = bacc.Bacc("TRN2", target_bir_lowering=False, num_devices=1)
    handles = [nc.dram_tensor(k, a.shape, mybir.dt.from_np(a.dtype), kind="ExternalInput").ap() for k, a in arrays.items()]
    out = nc.dram_tensor("out", (S, D), f32, kind="ExternalOutput").ap()
    build_trunk(nc, *handles, out)
    r = run_bass_kernel_spmd(nc, [arrays], core_ids=[0])
    return r.results[0]["out"].reshape(1, S, D)
```

```python
import concourse.bass as bass
from concourse import mybir
from concourse.alu_op_type import AluOpType as ALU

f32 = mybir.dt.float32
f32r = mybir.dt.float32r
i32 = mybir.dt.int32
u8 = mybir.dt.uint8
ACT = mybir.ActivationFunctionType
AX = mybir.AxisListType

P = 128
D = 2048
S = 256
TT = S // P
KT = D // P
PARTS = 4
UK, UC = 8, 256
HALVES = 9
QMEM, POOL, FGT, QRY, XS, BC, OGATE, VAL, ZG = range(HALVES)
UP = 2 * HALVES
DBLK = D // UC
UM = 12
N_X = 4
N_KV = 16
N_P0 = N_X + N_KV
N_M0 = N_P0 + PARTS * UP
N_O0 = N_M0 + DBLK * UM
N_S0 = N_O0 + 2 * DBLK
N_D0 = N_S0 + 4
N_UNITS = N_D0 + 2
START = 1
RAW, SPLIT = 3, 2

E = 64
TOPK, GROUPS, TOPG = 8, 8, 4
PAIRS = E // 2
CAP = 64
ROUTED_SCALE = 2.5
MASK_SCORE = -1e4
FE = 256
ALPHA = 2.0 ** 0.25
EPS = 1e-5
LEVELS = 9
NP = 28


def build_trunk(nc, units, params, hnorm, wdt, dtb, alog, poolm, poolw, xtok, lnp, wrt, rbias, wgu, wd, out):
    base = 16512

    def at(name, kb, shape, dt=f32):
        return nc.alloc_sbuf_tensor_at(name, shape, dt, offset=base + int(kb * 1024))

    xhi = at("xhi", 0, [P, KT, S], f32r)
    xlo = at("xlo", 16, [P, KT, S], f32r)
    raw = [at(f"raw{s}", 32 + 8 * s, [P, UK * UC]) for s in range(RAW)]
    whi = [at(f"whi{s}", 56 + 8 * s, [P, UK * UC], f32r) for s in range(SPLIT)]
    wlo = [at(f"wlo{s}", 72 + 8 * s, [P, UK * UC], f32r) for s in range(SPLIT)]
    ident = at("ident", 88, [P, P])
    later = at("later", 88.5, [P, P])
    upto = at("upto", 89, [P, P])
    before = at("before", 89.5, [P, P])
    ones = at("ones", 90, [P, P])
    quart = at("quart", 90.5, [P, 3, P])
    lmask = at("lmask", 92, [P, LEVELS - 2, P], u8)
    par = at("par", 93, [P, PARTS, NP])
    prm = at("prm", 93.5, [P, NP])
    hnw = at("hnw", 93.8125, [P, 8])
    hdt = at("hdt", 93.875, [P, TT, 16])
    ad = at("ad", 94, [P, TT, 16])
    small = at("small", 94.25, [P, 16, 8])
    kT = at("kT", 96, [P, 8, S])
    vmem = at("vmem", 104, [P, TT, 4 * UC])
    yT = at("yT", 112, [P, 4, 8, S])
    mhi = at("mhi", 144, [P, KT, S], f32r)
    mlo = at("mlo", 160, [P, KT, S], f32r)
    tok = [0.0]

    def tmp(name, shape, dt=f32, start=144):
        n = 1
        for d in shape[1:]:
            n *= d
        t = at(name, start + tok[0], shape, dt)
        tok[0] += (n * 4 + 31) // 32 * 32 / 1024
        assert start + tok[0] <= 207.8, (name, tok[0])
        return t

    poolmix = tmp("poolmix", [P, TT, S])
    poolwt = tmp("poolwt", [P, 2, UC])
    upool = tmp("upool", [P, TT, UC])
    dpool = tmp("dpool", [P, 2, S])
    qm = tmp("qm", [P, 2, S])
    vm = tmp("vm", [P, 2, UC])
    prob = tmp("prob", [P, TT, S])
    probT = tmp("probT", [P, 2, S])
    fgate = tmp("fgate", [P, 2 * S])
    fr = tmp("fr", [P, 2, S])
    kk = tmp("kk", [P, 2, S])
    qq = tmp("qq", [P, 2, S])
    blk = [fgate, tmp("blk2", [P, S])] + [tmp(f"blk{2 ** j}", [P, S >> (j - 1)]) for j in range(2, 8)]
    att = tmp("att", [P, 2 * TT, P])
    attx = tmp("attx", [P, 2, P])
    vh = tmp("vh", [P, TT, UC])
    gs = tmp("gs", [P, 2, S])
    th = tmp("th", [P, 2, S])
    up = tmp("up", [P, 4, 3 + S])
    cv = tmp("cv", [P, 4, S])
    tc = tmp("tc", [P, 4, S])
    xt = tmp("xt", [P, TT, UC])
    dec = tmp("dec", [P, 3, 4, P])
    ta = tmp("ta", [P, 3, 4, P])
    cbm = tmp("cbm", [P, 3, P])
    osq, rh, rs = th[:, :, :].rearrange("p a b -> p (a b)"), kk[:, :, :].rearrange("p a b -> p (a b)"), blk[1]
    zs, yss = fr, qq
    wdt_raw = at("wdt_raw", 176, [P, KT * 16])
    wdt_hi = at("wdt_hi", 177, [P, KT, 16], f32r)
    wdt_lo = at("wdt_lo", 178, [P, KT, 16], f32r)
    dtbias = at("dtbias", 179, [P, 32])
    aneg = at("aneg", 179.25, [P, 32])
    dts = at("dts", 179.5, [P, 8, 32])
    xi = at("xi", 181, [P, 2 * P], i32)
    xf = at("xf", 182, [P, 3, P])
    N_CONST = 14

    yhi = [at(f"yhi{n}", o, [P, UK, S], f32r) for n, o in enumerate((96, 144, 160, 176))]
    ylo = [at(f"ylo{n}", o + 8, [P, UK, S], f32r) for n, o in enumerate((96, 144, 160, 176))]
    ghi = at("merged_hi", 112, [P, KT, S], f32r)
    glo = at("merged_lo", 128, [P, KT, S], f32r)
    sig = at("sig", 192, [P, 4, 2 * S])
    macc = at("macc", 200, [P, 2 * S])
    mtmp = at("mtmp", 202, [P, 2 * S])
    htok = at("h", 144, [P, TT, D])
    lng = [at("ln1_gain", 96, [P, D]), at("ln2_gain", 64, [P, D])]
    lnb = [at("ln1_bias", 104, [P, D]), at("ln2_bias", 72, [P, D])]
    bns = at("bns", 204, [P, TT, 4, 6])
    bna = at("bna", 204.25, [P, TT, 2])
    bnr = at("bnr", 204.5, [P, TT, 4])
    wrt_raw = at("wrt_raw", 192, [P, KT, E])
    wrt_st = at("wrt_stacked", 196, [P, KT, 2 * E], f32r)
    hhi = at("hhi", 112, [P, KT, S], f32r)
    hlo = at("hlo", 128, [P, KT, S], f32r)
    stack_id = at("stack_id", 95.5, [P, E])
    rsum = at("rsum", 104.5, [P, S])
    sth = at("sth", 96, [P, 2 * S])
    sact = at("sact", 98, [P, 2 * S])
    shi = at("shi", 100, [P, 2, S], f32r)
    slo = at("slo", 102, [P, 2, S], f32r)
    EE = [P, TT, E]
    score, choice, masked, repl, sel, wsel, rtmp = (at(f"router{j}", 105.5 + j * 0.5, EE) for j in range(7))
    gmax = at("gmax", 109, [P, TT, GROUPS, 8])
    gsum = at("gsum", 109.5, [P, TT, GROUPS])
    gcmp = at("gcmp", 109.75, [P, TT, GROUPS, GROUPS])
    gcmp2 = at("gcmp2", 110.25, [P, TT, GROUPS, GROUPS])
    gmask = at("gmask", 110.75, [P, TT, GROUPS])
    gpen = at("gpen", 111, [P, TT, GROUPS])
    top8 = at("top8", 111.25, [P, TT, 8])
    wsum = at("wsum", 111.5, [P, TT, 2])
    rbias_t = at("router_bias", 95.25, [P, E])
    glt = at("group_before", 95, [P, GROUPS, GROUPS])
    acc = at("acc", 128, [P, TT, D])
    EP = E + 4
    rank = at("rank", 205.5, [P, TT, EP])
    wgt = at("wgt", 206.25, [P, TT, EP])
    slots = at("slots", 94.75, [P, CAP])
    rounds = at("rounds", 207.25, [P, 1], i32)
    rcnt = at("rcnt", 207.3125, [P, 4])
    wgu_t = [at("wgu0", 0, [P, 4, 4, 2 * FE]), at("wgu1", 160, [P, 4, 4, 2 * FE])]
    wd_t = [at("wd0", 112, [P, 2, D]), at("wd1", 96, [P, 2, D])]
    xg = at("xg", 32, [P, KT, 2 * CAP])
    yehi = at("ye_hi", 40, [P, D], f32r)
    yelo = at("ye_lo", 48, [P, D], f32r)
    pick = at("pick", 56, [P, TT, 2, CAP])
    pickw = at("pickw", 57, [P, TT, 2, CAP])
    pickT = at("pickT", 58, [P, TT, P], f32r)
    pickwT = at("pickwT", 62, [P, TT * P])
    wslot = at("wslot", 63, [P, 1])
    eth = at("eth", 59, [P, FE])
    eact = at("eact", 60, [P, FE])
    eactT = at("eactT", 61, [P, 2, P])

    bank = [nc.alloc_psum_tensor(f"bank{b}", [P, 512], f32) for b in range(8)]

    def sem(name):
        return nc.alloc_semaphore(name)

    raw_full = [sem(f"raw_full{s}") for s in range(RAW)]
    hi_done, lo_done, unit_used = sem("hi_done"), sem("lo_done"), sem("unit_used")
    par_in, const_ok, dt_in = sem("par_in"), sem("const_ok"), sem("dt_in")
    mem_read = sem("mem_read")
    lb_e, lb_x = sem("lb_ready"), sem("lb_exp")

    NH = 8

    def cnt(i, per, k):
        return i * per + k

    def half_count(p, h):
        return p * UP + (N_KV + 2 * h)

    def dense(pe, n, u, out_bank, act_hi, act_lo, kofs, first, last, tokens_stationary):
        hi, lo = whi[u % SPLIT], wlo[u % SPLIT]
        pe.wait_ge(lo_done, n + 1)
        m = None
        for t in range(2):
            for k in range(UK):
                wh, wl = (w[:, k * UC:(k + 1) * UC] for w in (hi, lo))
                xh, xl = act_hi[:, kofs + k, :], act_lo[:, kofs + k, :]
                for j, (w, x) in enumerate(((wh, xh), (wh, xl), (wl, xh))):
                    if tokens_stationary:
                        lhsT, rhs = x[:, t * P:(t + 1) * P], w
                    else:
                        lhsT, rhs = w[:, t * P:(t + 1) * P], x
                    m = nc.tensor.matmul(out_bank[:, t * UC:(t + 1) * UC], lhsT, rhs,
                                         start=first and t == 0 and k == 0 and j == 0,
                                         stop=last and k == UK - 1 and j == 2, skip_group_check=True)
        m.then_inc(unit_used, 1)
        return m

    names = ("u_ok pmix_in pw_in dp_ps dp_ok yp_ps yp_ok qm_ok vm_ok sc_ps nmx_ok p_ok pn_ok pt_ps pt_ok cx_ps cx_ok "
             "f_exp kk_ok qt_ok lev_ps lev_ok lev_k x_ps x_ok vh_ok gt_ok gs_ok o_ps osq_ok oss_ps ovar_ok osd_ok yh_ok "
             "up_ok cv_ok tc_ok xc_ok xtp_ps xt_ok cb_ps cb_ok ta_ok dec_ps dec_ok g_ok y_ps tz_ok y1_ok ysq_ok "
             "yss_ps yvar_ok ysd_ok ys_ok vch").split()
    s = {n: sem("part_" + n) for n in names}
    dt_ps, dt_e, dt_l, dt_a, dt_w = sem("dt_ps"), sem("dt_e"), sem("dt_l"), sem("dt_a"), sem("dt_w")
    upz = sem("up_zeroed")
    dt_chain = sem("dt_chain")
    mg = {n: sem("merge_" + n) for n in "y1_hi y1_lo y_hi y_lo gate_ok mul_ok block_ok ch".split()}
    og = {n: sem("out_" + n) for n in
         "x_in res_ok ln_in stats_ok sd_ok nrm_ok scaled_ok tr_ps hi_ok lo_ok ln_ch w_in whi_ok wlo_ok".split()}
    rt = {n: sem("router_" + n) for n in "ps sum_ok lg_ps exp_ok sel_ok rk_ps ch rounds_ok ready".split()}
    sh = {n: sem("shared_" + n) for n in "th_ok a_ok hi_ok lo_ok acc_ok ch dps".split()}
    ex = {n: sem("expert_" + n) for n in
         "gu_free wslot_ok y_split pick_ok pickw_ok ga_ps xg_act xg_dve gu_ps th_ok a_ok ch at_ps at_ok pt_ps pt_ok y_ps y_ok "
         "sc_ps acc_ok zero round_end out_ok g2".split()}
    gu_full = [sem(f"expert_gu_full{c}") for c in range(4)]
    d_full = [sem(f"expert_d_full{c}") for c in range(2)]
    VC = 35

    def unit_wait(i, per, b, u):
        assert per % RAW == 0
        return (i * (per // RAW) + (b + u) // RAW + 1) * 16

    blkctx = nc.Block()
    block = blkctx.__enter__()

    @block.sync
    def _(sp):
        for u in range(RAW):
            sp.dma_start(raw[u][:, :], units[u]).then_inc(raw_full[u], 16)
        sp.dma_start(wdt_raw[:, :], wdt).then_inc(dt_in, 16)
        sp.dma_start(par[:, :, :], params).then_inc(par_in, 16)
        sp.dma_start(hnw[:, 0:1], hnorm).then_inc(par_in, 16)
        sp.dma_start(dtbias[:, :], dtb).then_inc(par_in, 16)
        sp.dma_start(aneg[:, :], alog).then_inc(par_in, 16)
        with sp.Fori(1, N_UNITS // RAW) as r:
            for u in range(RAW):
                sp.wait_ge(hi_done, r * RAW + (u + 1 - RAW))
                sp.wait_ge(lo_done, r * RAW + (u + 1 - RAW))
                sp.dma_start(raw[u][:, :], units[r * RAW + u]).then_inc(raw_full[u], 16)

        def load_down(pair):
            for c in range(2):
                for j in range(2):
                    sp.dma_start(wd_t[j][:, c, :], wd[pair * 2 + j, c]).then_inc(d_full[c], 16)

        def load_pair(it, pair):
            for c in range(4):
                for j in range(2):
                    sp.wait_ge(ex["gu_free"], it * 4 + (c - 3) + START)
                    sp.dma_start(wgu_t[j][:, c, :, :], wgu[pair * 2 + j, c]).then_inc(gu_full[c], 16)
            sp.wait_ge(ex["y_ps"], it * 4 + START)
            load_down(pair)

        sp.wait_ge(sh["dps"], 8)
        sp.wait_ge(rt["rounds_ok"], 1)
        load_down(0)
        with sp.Fori(1, PAIRS) as pair:
            load_pair(pair, pair)
        n_rounds = sp.value_load(rounds[0:1, 0:1], min_val=1, max_val=4)
        with sp.If(n_rounds > 1):
            with sp.Fori(1, n_rounds) as b:
                with sp.Fori(0, PAIRS) as pair:
                    load_pair(b * PAIRS + pair, pair)
        for t in range(TT):
            for c in range(2):
                sp.wait_ge(og["scaled_ok"], 4 * TT + t * 4 + c * 2 + 2)
                sl = slice(c * 1024, (c + 1) * 1024)
                sp.dma_start(out[t * P:(t + 1) * P, sl], acc[:, t, sl]).then_inc(ex["out_ok"], 16)
        sp.wait_ge(ex["out_ok"], 32 * TT)

    started = [s[n] for n in "cv_ok cx_ps dec_ps dp_ps gs_ok kk_ok o_ps oss_ps p_ok pt_ps sc_ps vh_ok x_ok x_ps y1_ok "
                             "y_ps yh_ok yp_ps ys_ok yss_ps".split()]
    started += [mg[n] for n in "block_ok gate_ok mul_ok".split()] + [og["res_ok"]]
    started += [ex[n] for n in "a_ok acc_ok at_ps ga_ps gu_free pt_ok pt_ps xg_act xg_dve y_ok y_ps y_split".split()]

    @block.gpsimd
    def _(pool):
        for one in started:
            pool.sem_inc(one, START)
        chain = [0]

        def link(ins):
            chain[0] += 1
            ins.then_inc(const_ok, 1)
            pool.wait_ge(const_ok, chain[0])

        link(nc.gpsimd.memset(ones[:, :], 1.0))
        link(nc.gpsimd.memset(ident[:, :], 0.0))
        link(nc.gpsimd.memset(quart[:, :, :], 0.25))
        link(nc.gpsimd.affine_select(out=ident[:, :], in_=ident[:, :], compare_op=ALU.not_equal, fill=1.0, base=0,
                                     pattern=[[-1, P]], channel_multiplier=1))
        link(nc.gpsimd.affine_select(out=later[:, :], in_=ones[:, :], compare_op=ALU.is_gt, fill=0.0, base=0,
                                     pattern=[[-1, P]], channel_multiplier=1))
        link(nc.gpsimd.affine_select(out=upto[:, :], in_=ones[:, :], compare_op=ALU.is_ge, fill=0.0, base=0,
                                     pattern=[[1, P]], channel_multiplier=-1))
        link(nc.gpsimd.affine_select(out=before[:, :], in_=ones[:, :], compare_op=ALU.is_gt, fill=0.0, base=0,
                                     pattern=[[1, P]], channel_multiplier=-1))
        for b in (0, 2):
            link(nc.gpsimd.affine_select(out=quart[:, b, :], in_=quart[:, b, :], compare_op=ALU.is_ge, fill=0.0,
                                         base=0, pattern=[[1, P]], channel_multiplier=-1))
        link(nc.gpsimd.iota(xi[:, 0:P], [[1, P]], base=0, channel_multiplier=0))
        link(nc.gpsimd.iota(xi[:, P:2 * P], [[0, P]], base=0, channel_multiplier=1))
        link(nc.gpsimd.iota(slots[:, :], [[1, CAP]], base=0, channel_multiplier=0, allow_small_or_imprecise_dtypes=True))
        link(nc.gpsimd.memset(glt[:, :, :], 1.0))
        link(nc.gpsimd.affine_select(out=glt[:, :, :], in_=glt[:, :, :], compare_op=ALU.is_gt, fill=0.0, base=0,
                                     pattern=[[1, GROUPS], [-1, GROUPS]], channel_multiplier=0))
        assert chain[0] == N_CONST
        with pool.Fori(0, PARTS) as p:
            pool.wait_ge(s["cx_ps"], p + START)
            pool.wait_ge(mem_read, NH)
            pool.wait_ge(unit_used, 2 * NH)
            nc.gpsimd.tensor_copy(vm[:, :, :], vmem[:, :, bass.ts(p, UC)]).then_inc(s["vm_ok"], 1)

        for i, n in enumerate((0, 2, 3)):
            if n == 0:
                pool.wait_ge(s["yp_ok"], 2 * PARTS)
                pool.wait_ge(s["sc_ps"], PARTS + START)
                pool.wait_ge(s["vm_ok"], PARTS)
            if n == 2:
                pool.wait_ge(s["ys_ok"], 2 * PARTS + START)
                pool.wait_ge(s["yh_ok"], PARTS + START)
                pool.wait_ge(s["cx_ok"], PARTS)
                pool.wait_ge(s["yss_ps"], PARTS + START)
            nc.gpsimd.tensor_copy(yhi[n][:, :, :], yT[:, n, :, :]).then_inc(mg["y_hi"], 1)
            pool.wait_ge(mg["y_hi"], i + 1)
            nc.gpsimd.tensor_tensor(ylo[n][:, :, :], yT[:, n, :, :], yhi[n][:, :, :].bitcast(f32), ALU.subtract)\
                .then_inc(mg["y_lo"], 1)

        pool.dma_start(rbias_t[:, :], rbias.partition_broadcast(P)).then_inc(og["w_in"], 16)
        pool.wait_ge(mg["block_ok"], DBLK + START)
        pool.wait_ge(unit_used, N_O0 - N_X)
        for t in range(TT):
            pool.dma_start(htok[:, t, :], xtok[t * P:(t + 1) * P, :]).then_inc(og["x_in"], 16)
        pool.dma_start(wrt_raw[:, :, :], wrt).then_inc(og["w_in"], 16)
        pool.dma_start(lng[0][:, :], lnp[0].partition_broadcast(P)).then_inc(og["ln_in"], 16)
        pool.dma_start(lnb[0][:, :], lnp[1].partition_broadcast(P)).then_inc(og["ln_in"], 16)
        pool.wait_ge(unit_used, N_UNITS - N_X)
        pool.dma_start(lng[1][:, :], lnp[2].partition_broadcast(P)).then_inc(ex["g2"], 16)
        pool.dma_start(lnb[1][:, :], lnp[3].partition_broadcast(P)).then_inc(ex["g2"], 16)

    @block.tensor
    def _(pe):
        pe.wait_ge(lo_done, N_X)
        pe.wait_ge(const_ok, N_CONST)
        pe.wait_ge(dt_w, 2)
        for t in range(TT):
            for k in range(KT):
                for j, (x, w) in enumerate(((xhi, wdt_hi), (xlo, wdt_hi), (xhi, wdt_lo))):
                    m = nc.tensor.matmul(bank[7][:, 16 * t:16 * t + 16], x[:, k, t * P:(t + 1) * P], w[:, k, :],
                                         start=k == 0 and j == 0, stop=k == KT - 1 and j == 2)
        m.then_inc(dt_ps, 1)
        for h in range(NH):
            if h >= 3:
                pe.wait_ge(mem_read, h - 2)
            for j in range(2):
                n = N_X + 2 * h + j
                m = dense(pe, n, n, bank[h % 3], mhi, mlo, UK * j, j == 0, j == 1, h >= 4)
        pe.wait_ge(mem_read, NH - 1)
        for j in range(2):
            dense(pe, N_P0 + j, N_P0 + j, bank[0], xhi, xlo, UK * j, j == 0, j == 1, False)
        pe.wait_ge(mem_read, NH)
        with pe.Fori(0, PARTS) as p:
            def half(h, j):
                n = N_P0 + 2 * h + j
                if j == 0:
                    if h == HALVES:
                        pe.wait_ge(s["gs_ok"], p + 1 + START)
                    elif h == 1:
                        pe.wait_ge(s["vh_ok"], p + START)
                    elif h == 2:
                        pe.wait_ge(s["y1_ok"], p + START)
                    elif h == 3:
                        pe.wait_ge(s["qm_ok"], p + 1)
                    elif h == 4:
                        pe.wait_ge(s["u_ok"], p + 1)
                    elif h == 5:
                        pe.wait_ge(s["f_exp"], p + 1)
                    elif h == 6:
                        pe.wait_ge(s["lev_ok"], cnt(p, 17, 1))
                    elif h == 7:
                        pe.wait_ge(s["up_ok"], cnt(p, 2, 1))
                    elif h == 8:
                        pe.wait_ge(s["up_ok"], cnt(p, 2, 2))
                m = dense(pe, p * UP + n, n, bank[h % 3], xhi, xlo, UK * j, j == 0, j == 1, h in (POOL, VAL))

            def mm(o, a, b, start=True, stop=True, **kw):
                return nc.tensor.matmul(o, a, b, start=start, stop=stop, **kw)

            def level(l):
                if l == 0:
                    pe.wait_ge(s["kk_ok"], p + 1 + START)
                    pe.wait_ge(s["x_ok"], p + START)
                pe.wait_ge(s["lev_ok"], cnt(p, 17, 2 * l + 1))
                for h in range(2):
                    if l < LEVELS - 1:
                        for t in range(TT):
                            sl = slice(t * P, (t + 1) * P)
                            m = mm(bank[6][:, (2 * h + t) * P:(2 * h + t + 1) * P], kk[:, h, sl], qq[:, h, sl])
                    else:
                        m = mm(bank[6][:, h * P:(h + 1) * P], kk[:, h, 0:P], qq[:, h, P:S])
                m.then_inc(s["lev_ps"] if l < LEVELS - 1 else s["x_ps"], 1)

            half(1, 0)
            half(1, 1)
            half(2, 0)
            pe.wait_ge(s["u_ok"], p + 1)
            pe.wait_ge(s["pmix_in"], (p + 1) * 16)
            pe.wait_ge(s["yh_ok"], p + START)
            for c in range(2):
                for t in range(TT):
                    m = mm(bank[3][:, c * S:(c + 1) * S], upool[:, t, c * P:(c + 1) * P], poolmix[:, t, :],
                           t == 0, t == TT - 1)
            m.then_inc(s["dp_ps"], 1)
            pe.wait_ge(s["ta_ok"], 3 * p + 3)
            pe.wait_ge(s["y1_ok"], p + START)
            mm(bank[5][:, :], later[:, :], ta[:, 0, :, :].rearrange("p h l -> p (h l)")).then_inc(s["dec_ps"], 1)
            half(2, 1)
            pe.wait_ge(s["dec_ok"], cnt(p, 3, 1))
            mm(bank[5][:, :], later[:, :], ta[:, 1, :, :].rearrange("p h l -> p (h l)")).then_inc(s["dec_ps"], 1)
            pe.wait_ge(s["qm_ok"], p + 1)
            pe.wait_ge(s["ys_ok"], 2 * p + START)
            for t in range(TT):
                for k in range(2):
                    m = mm(bank[4][:, t * S:(t + 1) * S], qm[:, k, t * P:(t + 1) * P], kT[:, p * 2 + k, :],
                           k == 0, k == 1)
            m.then_inc(s["sc_ps"], 1)
            pe.wait_ge(s["dp_ok"], p + 1)
            pe.wait_ge(s["pw_in"], (p + 1) * 16)
            for c in range(2):
                for k in range(2):
                    m = mm(bank[3][:, c * S:(c + 1) * S], poolwt[:, k, c * P:(c + 1) * P], dpool[:, k, :],
                           k == 0, k == 1)
            m.then_inc(s["yp_ps"], 1)
            half(3, 0)
            pe.wait_ge(s["dec_ok"], cnt(p, 3, 2))
            mm(bank[5][:, :], later[:, :], ta[:, 2, :, :].rearrange("p h l -> p (h l)"), stop=False)
            mm(bank[5][:, :], ones[:, :], ta[:, 1, :, :].rearrange("p h l -> p (h l)"), start=False)\
                .then_inc(s["dec_ps"], 1)
            half(3, 1)
            half(4, 0)
            level(0)
            half(4, 1)
            level(1)
            pe.wait_ge(s["pn_ok"], p + 1)
            for mt in range(2):
                for t in range(TT):
                    m = nc.tensor.transpose(bank[4][:, mt * S + t * P:mt * S + (t + 1) * P],
                                            prob[:, t, mt * P:(mt + 1) * P], ident[:, :])
            m.then_inc(s["pt_ps"], 1)
            half(5, 0)
            level(2)
            half(5, 1)
            level(3)
            pe.wait_ge(s["pt_ok"], p + 1)
            pe.wait_ge(s["vm_ok"], p + 1)
            pe.wait_ge(s["yp_ok"], 2 * p + 2)
            for c in range(2):
                for mt in range(2):
                    m = mm(bank[3][:, c * S:(c + 1) * S], vm[:, mt, c * P:(c + 1) * P], probT[:, mt, :],
                           mt == 0, mt == 1)
            m.then_inc(s["cx_ps"], 1)
            half(6, 0)
            level(4)
            half(6, 1)
            level(5)
            pe.wait_ge(s["xc_ok"], cnt(p, 2, 1))
            for t in range(TT):
                for c in range(2):
                    m = nc.tensor.transpose(bank[4][:, t * UC + c * P:t * UC + (c + 1) * P],
                                            cv[:, c, t * P:(t + 1) * P], ident[:, :])
            m.then_inc(s["xtp_ps"], 1)
            half(7, 0)
            level(6)
            half(7, 1)
            level(7)
            pe.wait_ge(s["xc_ok"], cnt(p, 2, 2))
            pe.wait_ge(s["cx_ok"], p + 1)
            mm(bank[3][:, 0:S], cv[:, 2, 0:P], cv[:, 3, :])
            mm(bank[3][:, S:S + P], cv[:, 2, P:S], cv[:, 3, P:S]).then_inc(s["cb_ps"], 1)
            half(8, 0)
            level(8)
            half(8, 1)
            half(HALVES, 0)
            pe.wait_ge(s["g_ok"], p + 1)
            pe.wait_ge(s["xt_ok"], 2 * p + 2)
            for c in range(2):
                for (l, terms) in ((0, ((0, 0),)), (1, ((0, 1), (1, 2)))):
                    for i, (t, b) in enumerate(terms):
                        for r in range(2):
                            h = 2 * c + r
                            m = mm(bank[5][64 * r:64 * r + 64, c * S + l * P:c * S + (l + 1) * P],
                                   xt[:, t, 64 * h:64 * h + 64], dec[:, b, h, :], i == 0, i == len(terms) - 1)
            m.then_inc(s["y_ps"], 1)
            pe.wait_ge(s["x_ok"], p + 1 + START)
            pe.wait_ge(s["vh_ok"], p + 1 + START)
            pe.wait_ge(s["lev_ok"], cnt(p, 17, 17))
            for h in range(2):
                vs = [vh[:, t, h * P:(h + 1) * P] for t in range(TT)]
                mm(bank[7][:, h * S:h * S + P], vs[0], att[:, 2 * h, :])
                mm(bank[7][:, h * S + P:(h + 1) * S], vs[1], att[:, 2 * h + 1, :], stop=False)
                m = mm(bank[7][:, h * S + P:(h + 1) * S], vs[0], attx[:, h, :], start=False)
            m.then_inc(s["o_ps"], 1)
            half(HALVES, 1)
            pe.wait_ge(s["osq_ok"], p + 1)
            pe.wait_ge(s["cb_ok"], p + 1)
            mm(bank[3][:, :], ones[:, :], osq).then_inc(s["oss_ps"], 1)
            pe.wait_ge(s["ysq_ok"], p + 1)
            mm(bank[4][:, 0:S], ones[:, :], tc[:, 0, :], stop=False)
            mm(bank[4][:, 0:S], ones[:, :], tc[:, 1, :], start=False).then_inc(s["yss_ps"], 1)


        def merge_block(b, units_to):
            for u in range(2, units_to):
                n, j = u // 3, u % 3
                if u == 2:
                    pe.wait_ge(s["vh_ok"], PARTS + START)
                if u == 3:
                    pe.wait_ge(s["y1_ok"], PARTS + START)
                    pe.wait_ge(mg["gate_ok"], b * 4 + START)
                if u == 5:
                    pe.wait_ge(s["ys_ok"], 2 * PARTS + START)
                    pe.wait_ge(s["yh_ok"], PARTS + START)
                    pe.wait_ge(mg["mul_ok"], b * 4 + START)
                if u == 11:
                    pe.wait_ge(mg["mul_ok"], b * 4 + 1 + START)
                if u == UM:
                    pe.wait_ge(mg["gate_ok"], b * 4 + 1 + START)
                if j < 2:
                    dense(pe, b * UM + (N_M0 + u), N_M0 + u, bank[2 * n % 8], xhi, xlo, UK * j, j == 0, j == 1, False)
                else:
                    if n == 1:
                        pe.wait_ge(mg["y1_lo"], 1)
                    else:
                        pe.wait_ge(mg["y_lo"], (1, None, 2, 3)[n])
                    dense(pe, b * UM + (N_M0 + u), N_M0 + u, bank[2 * n + 1], yhi[n], ylo[n], 0, True, True, False)

        with pe.Fori(0, DBLK - 1) as b:
            merge_block(b, UM + 2)
        merge_block(DBLK - 1, UM)

        pe.wait_ge(mg["block_ok"], DBLK // 2 + START)
        pe.wait_ge(mg["gate_ok"], 4 * DBLK + START)

        def out_half(i, c, u0):
            for j in range(2):
                if j == 1:
                    pe.wait_ge(mg["block_ok"], DBLK + START)
                dense(pe, i + (N_O0 + u0 + j), N_O0 + u0 + j, bank[u0 // 2 % 3], ghi, glo, UK * j, j == 0, j == 1, True)

        with pe.Fori(0, 2) as r3:
            for c in range(3):
                if c == 1:
                    pe.wait_ge(og["res_ok"], r3 * 3 + START)
                if c == 2:
                    pe.wait_ge(og["res_ok"], r3 * 3 + 1 + START)
                out_half(r3 * 6, c, 2 * c)
        for c in range(2):
            if c == 1:
                pe.wait_ge(og["res_ok"], 6 + START)
            out_half(12, c, 2 * c)

        for k2 in range(KT // 2):
            b = bank[3 + k2 % 4]
            pe.wait_ge(og["scaled_ok"], (k2 // 2 + 1) * TT)
            if k2 >= 4:
                pe.wait_ge(og["lo_ok"], k2 - 3)
            for j in range(2):
                for t in range(TT):
                    k = 2 * k2 + j
                    mi = nc.tensor.transpose(b[:, j * S + t * P:j * S + (t + 1) * P], htok[:, t, k * P:(k + 1) * P], ident[:, :])
            mi.then_inc(og["tr_ps"], 1)
        pe.wait_ge(og["lo_ok"], KT // 2)
        pe.wait_ge(og["wlo_ok"], 1)
        for k in range(KT):
            for j, xx in enumerate((hhi, hlo)):
                mi = nc.tensor.matmul(bank[7][:, 0:S], wrt_st[:, k, :], xx[:, k, :], start=k == 0 and j == 0,
                                      stop=k == KT - 1 and j == 1)
        mi.then_inc(rt["ps"], 1)
        for c in range(2):
            for j in range(2):
                n = N_S0 + 2 * c + j
                dense(pe, n, n, bank[c], hhi, hlo, UK * j, j == 0, j == 1, False)
            if c == 0:
                pe.wait_ge(rt["sum_ok"], 1)
                for t in range(TT):
                    mi = nc.tensor.matmul(bank[7][:, S + t * E:S + (t + 1) * E], rsum[:, t * P:(t + 1) * P], stack_id[:, :],
                                          start=True, stop=True)
                mi.then_inc(rt["lg_ps"], 1)
        pe.wait_ge(sh["lo_ok"], 1)
        for j in range(2):
            n = N_D0 + j
            pe.wait_ge(lo_done, n + 1)
            for t in range(TT):
                for c in range(2):
                    i = 4 * j + 2 * t + c
                    b = bank[2 + i % 5]
                    if i >= 5:
                        pe.wait_ge(sh["acc_ok"], i - 4)
                    for f in range(2):
                        sl = slice(f * 1024 + c * 512, f * 1024 + (c + 1) * 512)
                        for jj, (a, w) in enumerate(((shi, whi), (slo, whi), (shi, wlo))):
                            mi = nc.tensor.matmul(b[:, :], a[:, f, t * P:(t + 1) * P], w[n % SPLIT][:, sl],
                                                  start=f == 0 and jj == 0, stop=f == 1 and jj == 2)
                    mi.then_inc(sh["dps"], 1)
                    if i == 5:
                        pe.wait_ge(rt["sel_ok"], 1)
                        nc.tensor.matmul(bank[7][:, 0:E], before[:, :], sel[:, 0, :], start=True, stop=True)
                        nc.tensor.matmul(bank[7][:, E:2 * E], before[:, :], sel[:, 1, :], start=True, stop=False)
                        nc.tensor.matmul(bank[7][:, E:2 * E], ones[:, :], sel[:, 0, :], start=False, stop=True)
                        nc.tensor.matmul(bank[7][:, 2 * E:3 * E], ones[:, :], sel[:, 0, :], start=True, stop=False)
                        nc.tensor.matmul(bank[7][:, 2 * E:3 * E], ones[:, :], sel[:, 1, :], start=False, stop=True).then_inc(rt["rk_ps"], 1)
        pe.wait_ge(sh["dps"], 8)
        pe.sem_inc(unit_used, 2)
        pe.wait_ge(rt["rounds_ok"], 1)
        pe.wait_ge(sh["acc_ok"], 8)
        n_rounds = pe.value_load(rounds[0:1, 0:1], min_val=1, max_val=4)
        with pe.Fori(0, n_rounds) as b:
            def gather(g):
                pe.wait_ge(ex["pick_ok"], b * (PAIRS + 2) + (g + 1))
                for k4 in range(4):
                    pe.wait_ge(ex[("xg_act", "xg_dve")[k4 % 2]], b * (2 * PAIRS + 2) + (g * 2 + k4 // 2) + START)
                    for k in range(4):
                        for t in range(TT):
                            mi = nc.tensor.matmul(bank[k4 % 2][:, k * P:(k + 1) * P],
                                                  htok[:, t, (4 * k4 + k) * P:(4 * k4 + k + 1) * P],
                                                  pick[:, t, :, :].rearrange("p j s -> p (j s)"),
                                                  start=t == 0, stop=t == TT - 1)
                    mi.then_inc(ex["ga_ps"], 1)

            def scatter(i):
                for t in range(TT):
                    for c in range(4):
                        pe.wait_ge(ex["acc_ok"], b * (8 * PAIRS + 8) + i * 8 + max(0, 4 * t + c - 1) + START)
                        for j, y in enumerate((yehi, yelo)):
                            mi = nc.tensor.matmul(bank[6 + c % 2][:, :], pickT[:, t, :], y[:, c * 512:(c + 1) * 512],
                                                  start=j == 0, stop=j == 1)
                        mi.then_inc(ex["sc_ps"], 1)

            gather(0)
            with pe.Fori(0, PAIRS) as pair:
                it = b * PAIRS + pair
                pe.wait_ge(ex["xg_act"], b * (2 * PAIRS + 2) + (pair * 2 + 2) + START)
                pe.wait_ge(ex["xg_dve"], b * (2 * PAIRS + 2) + (pair * 2 + 2) + START)
                pe.wait_ge(ex["a_ok"], it + START)
                for c in range(4):
                    pe.wait_ge(gu_full[c], it * 32 + 32)
                    for k in range(4):
                        for j in range(2):
                            mi = nc.tensor.matmul(bank[3][CAP * j:CAP * j + CAP, :], xg[:, 4 * c + k, CAP * j:CAP * j + CAP],
                                                  wgu_t[j][:, c, k, :], start=c == 0 and k == 0, stop=c == 3 and k == 3)
                    mi.then_inc(ex["gu_free"], 1)
                gather(pair + 1)
                pe.wait_ge(ex["a_ok"], it + 1 + START)
                pe.wait_ge(ex["pt_ok"], it + START)
                for f in range(2):
                    mi = nc.tensor.transpose(bank[2][:, f * P:(f + 1) * P], eact[:, f * P:(f + 1) * P], ident[:, :])
                mi.then_inc(ex["at_ps"], 1)
                pe.wait_ge(ex["zero"], b * 3 + 3)
                pe.wait_ge(ex["y_split"], it * 4 + START)
                scatter(pair)
                pe.wait_ge(ex["pickw_ok"], it + 1)
                pe.wait_ge(ex["at_ok"], it + 1)
                for t in range(TT):
                    mi = nc.tensor.transpose(bank[2][:, S + t * P:S + (t + 1) * P],
                                             pickw[:, t, :, :].rearrange("p j s -> p (j s)"), ident[:, :])
                mi.then_inc(ex["pt_ps"], 1)
                for c in range(4):
                    pe.wait_ge(ex["y_split"], it * 4 + max(0, c - 1) + START)
                    for f in range(2):
                        pe.wait_ge(d_full[f], it * 32 + 32)
                        for j in range(2):
                            mi = nc.tensor.matmul(bank[4 + c % 2][CAP * j:CAP * j + CAP, :], eactT[:, f, CAP * j:CAP * j + CAP],
                                                  wd_t[j][:, f, c * 512:(c + 1) * 512], start=f == 0, stop=f == 1)
                    mi.then_inc(ex["y_ps"], 1)
            pe.wait_ge(ex["y_split"], b * (4 * PAIRS) + 4 * PAIRS + START)
            pe.wait_ge(ex["pt_ok"], b * PAIRS + PAIRS + START)
            scatter(PAIRS)

    @block.scalar
    def _(act):
        for n in range(N_X):
            dst = (xhi, mhi)[n // 2]
            act.wait_ge(raw_full[n % RAW], (n // RAW + 1) * 16)
            nc.scalar.activation(dst[:, UK * (n % 2):UK * (n % 2) + UK, :].rearrange("p k t -> p (k t)"),
                                 raw[n % RAW][:, :], ACT.Copy).then_inc(hi_done, 1)
        act.wait_ge(dt_in, 16)
        nc.scalar.activation(wdt_hi[:, :, :].rearrange("p k t -> p (k t)"), wdt_raw[:, :], ACT.Copy).then_inc(dt_w, 1)

        def hi(n, u, count):
            act.wait_ge(raw_full[u % RAW], count)
            act.wait_ge(unit_used, n - N_X - SPLIT + 1)
            nc.scalar.activation(whi[u % SPLIT][:, :], raw[u % RAW][:, :], ACT.Copy).then_inc(hi_done, 1)

        def hi_first(n):
            act.wait_ge(raw_full[n % RAW], (n // RAW + 1) * 16)
            nc.scalar.activation(whi[n % SPLIT][:, :], raw[n % RAW][:, :], ACT.Copy).then_inc(hi_done, 1)

        for n in (N_X, N_X + 1):
            hi_first(n)
        act.wait_ge(par_in, 64)
        nc.scalar.activation(dts[:, 7, :], aneg[:, :], ACT.Exp).then_inc(dt_a, 1)
        act.wait_ge(dt_e, 1)
        nc.scalar.activation(dts[:, 2, :], dts[:, 1, :], ACT.Exp).then_inc(dt_l, 1)
        act.wait_ge(dt_e, 2)
        nc.scalar.activation(dts[:, 4, :], dts[:, 3, :], ACT.Ln).then_inc(dt_l, 1)
        act.wait_ge(lb_e, 1)
        nc.scalar.activation(small[:, 1, :], small[:, 0, :], ACT.Exp).then_inc(lb_x, 1)
        for h in range(NH):
            for j in range(2):
                n = N_X + 2 * h + 2 + j
                hi(n, n, (n // RAW + 1) * 16)
            act.wait_ge(unit_used, 2 * h + 2)
            if h < 4:
                o = kT[:, 2 * h:2 * h + 2, :]
            else:
                o = vmem[:, :, (h - 4) * UC:(h - 3) * UC]
            nc.scalar.activation(o, bank[h % 3][:, :].rearrange("p (t c) -> p t c", t=2), ACT.Copy).then_inc(mem_read, 1)
        for n in range(N_P0 + 2, N_P0 + 5):
            hi(n, n, (n // RAW + 1) * 16)
        with act.Fori(0, PARTS) as p:
            def b3(b):
                return bank[b][:, :].rearrange("p (t c) -> p t c", t=2)

            for u in range(4, UP + 5):
                if u > 4:
                    n = N_P0 + u
                    hi(p * UP + n, n, unit_wait(p, UP, N_P0, u))
                if u == 4:
                    act.wait_ge(s["dp_ps"], p + START)
                    act.wait_ge(unit_used, 2 * NH)
                    act.dma_start(poolmix[:, :, :], poolm[p]).then_inc(s["pmix_in"], 16)
                    act.wait_ge(s["yp_ps"], p + START)
                    act.dma_start(poolwt[:, :, :], poolw[p]).then_inc(s["pw_in"], 16)
                if u == 4:
                    act.wait_ge(unit_used, half_count(p, 1))
                    act.wait_ge(s["sc_ps"], p + START)
                    nc.scalar.activation(qm[:, :, :], b3(0), ACT.Copy).then_inc(s["qm_ok"], 1)
                if u == 4:
                    act.wait_ge(unit_used, half_count(p, 2))
                    act.wait_ge(s["dp_ps"], p + START)
                    nc.scalar.activation(upool[:, :, :], b3(1), ACT.Copy).then_inc(s["u_ok"], 1)
                if u == 5:
                    act.wait_ge(s["dp_ps"], p + 1 + START)
                    act.wait_ge(s["yp_ps"], p + START)
                    nc.scalar.activation(dpool[:, :, :], b3(3), ACT.Copy).then_inc(s["dp_ok"], 1)
                if 5 <= u < 8:
                    b = (0, 2, 1)[u - 5]
                    act.wait_ge(s["dec_ps"], cnt(p, 3, u - 4) + START)
                    act.wait_ge(s["y_ps"], p + START)
                    nc.scalar.activation(dec[:, b, :, :], bank[5][:, :].rearrange("p (h l) -> p h l", h=4), ACT.Exp)\
                        .then_inc(s["dec_ok"], 1)
                if u == 6:
                    act.wait_ge(unit_used, half_count(p, 3))
                    act.wait_ge(s["kk_ok"], p + START)
                    nc.scalar.activation(fr[:, :, :], b3(2), ACT.Exp).then_inc(s["f_exp"], 1)
                    act.wait_ge(s["nmx_ok"], p + 1)
                    act.wait_ge(s["pt_ps"], p + START)
                    for t in range(TT):
                        nc.scalar.activation(prob[:, t, :], bank[4][:, t * S:(t + 1) * S], ACT.Exp,
                                             bias=small[:, 1, t:t + 1], scale=UC ** -0.5,
                                             accum_out=small[:, 2, t:t + 1]).then_inc(s["p_ok"], 1)
                if u == 8:
                    act.wait_ge(unit_used, half_count(p, 4))
                    act.wait_ge(s["oss_ps"], p + START)
                    nc.scalar.activation(th[:, :, :], b3(0), ACT.Tanh, scale=0.5).then_inc(s["qt_ok"], 1)
                if u == 10:
                    act.wait_ge(unit_used, half_count(p, 5))
                    act.wait_ge(s["cv_ok"], 2 * p + START)
                    act.wait_ge(upz, 1)
                    nc.scalar.activation(up[:, 0:2, 3:3 + S], b3(1), ACT.Copy).then_inc(s["up_ok"], 1)
                    act.wait_ge(s["pt_ps"], p + 1 + START)
                    act.wait_ge(s["cx_ps"], p + START)
                    nc.scalar.activation(probT[:, :, :], b3(4), ACT.Copy).then_inc(s["pt_ok"], 1)
                if u == 12:
                    act.wait_ge(unit_used, half_count(p, 6))
                    nc.scalar.activation(up[:, 2:4, 3:3 + S], b3(2), ACT.Copy).then_inc(s["up_ok"], 1)
                    act.wait_ge(s["cv_ok"], cnt(p, 2, 1) + START)
                    act.wait_ge(s["yss_ps"], p + START)
                    nc.scalar.activation(tc[:, 0:2, :], cv[:, 0:2, :], ACT.Tanh, scale=0.5).then_inc(s["tc_ok"], 1)
                    act.wait_ge(s["cx_ps"], p + 1 + START)
                    nc.scalar.activation(yT[:, 3, bass.ts(p, 2), :], b3(3), ACT.Copy).then_inc(s["cx_ok"], 1)
                if u == 14:
                    act.wait_ge(unit_used, half_count(p, 7))
                    act.wait_ge(s["lev_ok"], cnt(p, 17, 1))
                    nc.scalar.activation(th[:, :, :], b3(0), ACT.Tanh, scale=0.5).then_inc(s["gt_ok"], 1)
                    act.wait_ge(s["cv_ok"], cnt(p, 2, 2) + START)
                    nc.scalar.activation(tc[:, 2:4, :], cv[:, 2:4, :], ACT.Tanh, scale=0.5).then_inc(s["tc_ok"], 1)
                if u == 16:
                    act.wait_ge(unit_used, half_count(p, 8))
                    act.wait_ge(s["o_ps"], p + START)
                    nc.scalar.activation(vh[:, :, :], b3(1), ACT.Copy).then_inc(s["vh_ok"], 1)
                if u == 17:
                    act.wait_ge(s["x_ps"], p + 1 + START)
                    nc.scalar.activation(attx[:, :, :], bank[6][:, 0:2 * P].rearrange("p (h l) -> p h l", h=2), ACT.Copy)\
                        .then_inc(s["x_ok"], 1)
                if u == 18:
                    act.wait_ge(unit_used, half_count(p, 9))
                    nc.scalar.activation(zs[:, :, :], b3(2), ACT.Tanh, scale=0.5).then_inc(s["tz_ok"], 1)
                if u == 19:
                    act.wait_ge(s["o_ps"], p + 1 + START)
                    nc.scalar.activation(osq, bank[7][:, :], ACT.Square).then_inc(s["osq_ok"], 1)
                if u == 20:
                    act.wait_ge(s["y1_ok"], p + 1 + START)
                    nc.scalar.activation(tc[:, 0:2, :], yss[:, :, :], ACT.Square).then_inc(s["ysq_ok"], 1)
                    act.wait_ge(s["ovar_ok"], p + 1)
                    nc.scalar.activation(rh, rh, ACT.Sqrt).then_inc(s["osd_ok"], 1)
                    act.wait_ge(s["yvar_ok"], p + 1)
                    nc.scalar.activation(rs[:, :], rs[:, :], ACT.Sqrt).then_inc(s["ysd_ok"], 1)


        act.wait_ge(s["ys_ok"], 2 * PARTS + START)
        act.wait_ge(s["yh_ok"], PARTS + START)
        act.wait_ge(s["yss_ps"], PARTS + START)
        act.wait_ge(s["cx_ok"], PARTS)
        nc.scalar.activation(yhi[1][:, :, :], yT[:, 1, :, :], ACT.Copy).then_inc(mg["y1_hi"], 1)
        with act.Fori(0, DBLK) as b:
            for u in range(4, UM + 5):
                n = N_M0 + u
                if u > 4:
                    hi(b * UM + n, n, unit_wait(b, UM, N_M0, u))
                if u in (4, 5, 8, 11):
                    act.wait_ge(unit_used, b * UM + (N_M0 + (4, 5, 8, 11).index(u) * 3 + 2 - N_X))
                    if u == 4:
                        act.wait_ge(mg["mul_ok"], b * 4 + START)
                    g = (4, 5, 8, 11).index(u)
                    nc.scalar.activation(sig[:, g, :], bank[2 * g][:, :], ACT.Tanh, scale=0.5)\
                        .then_inc(mg["gate_ok"], 1)
        act.wait_ge(unit_used, N_O0 - N_X)
        for u in range(5, 16):
            n = N_O0 + u
            hi(n, n, (n // RAW + 1) * 16)
            if u % 4 == 1:
                for j in range(2):
                    act.dma_start(wgu_t[j][:, u // 4 - 1, :, :], wgu[j, u // 4 - 1]).then_inc(gu_full[u // 4 - 1], 16)
        for j in range(2):
            act.dma_start(wgu_t[j][:, 3, :, :], wgu[j, 3]).then_inc(gu_full[3], 16)

        def norm_part(k):
            act.wait_ge(og["stats_ok"], k + 1)
            nc.scalar.activation(bnr[:, :, 1:2], bnr[:, :, 0:1], ACT.Sqrt).then_inc(og["sd_ok"], 1)

        act.wait_ge(og["w_in"], 32)
        nc.scalar.activation(wrt_st[:, :, 0:E], wrt_raw[:, :, :], ACT.Copy).then_inc(og["whi_ok"], 1)
        norm_part(0)
        for k2 in range(KT // 2):
            act.wait_ge(og["tr_ps"], k2 + 1)
            nc.scalar.activation(hhi[:, 2 * k2:2 * k2 + 2, :], bank[3 + k2 % 4][:, :].rearrange("p (k t) -> p k t", k=2),
                                 ACT.Copy).then_inc(og["hi_ok"], 1)
        for n in (N_S0, N_S0 + 1):
            hi(n, n, (n // RAW + 1) * 16)
        act.wait_ge(rt["ps"], 1)
        nc.scalar.activation(rsum[:, :], bank[7][:, 0:S], ACT.Copy).then_inc(rt["sum_ok"], 1)
        for n in (N_S0 + 2, N_S0 + 3):
            hi(n, n, (n // RAW + 1) * 16)
        act.wait_ge(rt["lg_ps"], 1)
        nc.scalar.activation(score[:, :, :], bank[7][:, S:S + TT * E].rearrange("p (t e) -> p t e", t=TT), ACT.Exp,
                             scale=-1.0).then_inc(rt["exp_ok"], 1)
        hi(N_D0, N_D0, (N_D0 // RAW + 1) * 16)
        act.wait_ge(unit_used, N_D0 - 2 - N_X)
        nc.scalar.activation(sth[:, :], bank[0][:, :], ACT.Tanh, scale=0.5).then_inc(sh["th_ok"], 1)
        hi(N_D0 + 1, N_D0 + 1, ((N_D0 + 1) // RAW + 1) * 16)
        act.wait_ge(sh["a_ok"], 1)
        nc.scalar.activation(shi[:, :, :], sact[:, :].rearrange("p (c t) -> p c t", c=2), ACT.Copy).then_inc(sh["hi_ok"], 1)

        act.wait_ge(rt["rounds_ok"], 1)
        n_rounds = act.value_load(rounds[0:1, 0:1], min_val=1, max_val=4)
        with act.Fori(0, n_rounds) as b:
            def gathered(g, gu):
                act.wait_ge(ex["gu_free"], gu * 4 + START)
                for k4 in (0, 2):
                    act.wait_ge(ex["ga_ps"], b * (4 * PAIRS + 4) + (g * 4 + k4 + 1) + START)
                    nc.scalar.activation(xg[:, 4 * k4:4 * k4 + 4, :], bank[0][:, :].rearrange("p (k s) -> p k s", k=4),
                                         ACT.Copy).then_inc(ex["xg_act"], 1)

            gathered(0, b * PAIRS)
            with act.Fori(0, PAIRS) as pair:
                it = b * PAIRS + pair
                act.wait_ge(ex["gu_free"], it * 4 + 4 + START)
                nc.scalar.activation(eth[:, :], bank[3][:, 0:FE], ACT.Tanh, scale=0.5).then_inc(ex["th_ok"], 1)
                gathered(pair + 1, it + 1)
                act.wait_ge(ex["at_ps"], it + 1 + START)
                act.wait_ge(ex["y_ps"], it * 4 + START)
                nc.scalar.activation(eactT[:, :, :], bank[2][:, 0:S].rearrange("p (f s) -> p f s", f=2), ACT.Copy)\
                    .then_inc(ex["at_ok"], 1)
                act.wait_ge(ex["pt_ps"], it + 1 + START)
                act.wait_ge(ex["y_split"], it * 4 + START)
                nc.scalar.activation(pickwT[:, :], bank[2][:, S:2 * S], ACT.Copy, accum_out=wslot[:, :])\
                    .then_inc(ex["wslot_ok"], 1)
                act.wait_ge(ex["wslot_ok"], it + 1)
                act.wait_ge(ex["sc_ps"], b * (8 * PAIRS + 8) + (pair * 8 + 8))
                for c in range(4):
                    act.wait_ge(ex["y_ps"], it * 4 + (c + 1) + START)
                    nc.scalar.activation(yehi[:, c * 512:(c + 1) * 512], bank[4 + c % 2][:, :], ACT.Copy,
                                         scale=wslot[:, :]).then_inc(ex["y_ok"], 1)
        norm_part(1)

    @block.vector
    def _(dve):
        V = nc.vector

        def lo(u, n, dst=None, src_hi=None):
            dve.wait_ge(hi_done, n + 1)
            V.tensor_tensor(wlo[u % SPLIT][:, :], raw[u % RAW][:, :], whi[u % SPLIT][:, :].bitcast(f32),
                            ALU.subtract).then_inc(lo_done, 1)

        for n in range(N_X):
            h, l = ((xhi, xlo), (mhi, mlo))[n // 2]
            sl = slice(UK * (n % 2), UK * (n % 2) + UK)
            dve.wait_ge(hi_done, n + 1)
            V.tensor_tensor(l[:, sl, :].rearrange("p k t -> p (k t)"), raw[n % RAW][:, :],
                            h[:, sl, :].rearrange("p k t -> p (k t)").bitcast(f32), ALU.subtract).then_inc(lo_done, 1)
        dve.wait_ge(dt_w, 1)
        V.tensor_tensor(wdt_lo[:, :, :].rearrange("p k t -> p (k t)"), wdt_raw[:, :],
                        wdt_hi[:, :, :].rearrange("p k t -> p (k t)").bitcast(f32), ALU.subtract).then_inc(dt_w, 1)
        lo(N_X, N_X)
        lo(N_X + 1, N_X + 1)

        chain = [0]

        def link(ins):
            chain[0] += 1
            ins.then_inc(dt_chain, 1)
            dve.wait_ge(dt_chain, chain[0])

        dve.wait_ge(const_ok, N_CONST)
        link(V.tensor_tensor(xi[:, 0:P], xi[:, 0:P], xi[:, P:2 * P], ALU.bitwise_xor))
        link(V.tensor_copy(xf[:, 0, :], xi[:, 0:P]))
        link(V.tensor_tensor(xf[:, 0, :], xf[:, 0, :], before[:, :], ALU.mult))
        link(V.tensor_scalar(xf[:, 1, :], xf[:, 0, :], 1.0, None, ALU.is_ge))
        for k in range(LEVELS - 2):
            a, b = xf[:, 1 + k % 2, :], xf[:, 1 + (k + 1) % 2, :]
            link(V.tensor_scalar(b, xf[:, 0, :], float(2 ** (k + 1)), None, ALU.is_ge))
            link(V.tensor_tensor(lmask[:, k, :], a, b, ALU.subtract))
        dve.wait_ge(par_in, 64)
        dve.wait_ge(dt_ps, 1)
        v, ab, e1, u1, ln1, w1, m1, aa = (dts[:, j, :] for j in range(8))
        link(V.tensor_tensor(v, bank[7][:, 0:32], dtbias[:, :], ALU.add))
        link(V.tensor_scalar(ab, v, -1.0, None, ALU.mult))
        ins = V.tensor_tensor(ab, v, ab, ALU.min)
        ins.then_inc(dt_e, 1)
        dve.wait_ge(dt_l, 1)
        ins = V.tensor_scalar(u1, e1, 1.0, None, ALU.add)
        ins.then_inc(dt_e, 1)
        dve.wait_ge(dt_e, 2)
        link(V.tensor_scalar(w1, u1, 1.0, None, ALU.subtract))
        link(V.tensor_scalar(m1, w1, 0.0, None, ALU.is_equal))
        link(V.tensor_tensor(w1, w1, m1, ALU.add))
        link(V.reciprocal(w1, w1))
        link(V.tensor_tensor(w1, w1, e1, ALU.mult))
        dve.wait_ge(dt_l, 2)
        link(V.tensor_tensor(w1, w1, ln1, ALU.mult))
        link(V.tensor_tensor(m1, m1, e1, ALU.mult))
        link(V.tensor_tensor(w1, w1, m1, ALU.add))
        link(V.tensor_scalar(v, v, 0.0, None, ALU.max))
        link(V.tensor_tensor(v, v, w1, ALU.add))
        lbs, t0, t1 = par[:, :, 24:26], small[:, 0, :].rearrange("p (a b) -> p a b", b=2), \
            small[:, 1, :].rearrange("p (a b) -> p a b", b=2)
        V.tensor_tensor(t0, lbs, lbs, ALU.subtract).then_inc(lb_e, 1)
        dve.wait_ge(lb_x, 1)
        link(V.reciprocal(t0, t1))
        link(V.tensor_tensor(t0, t0, t1, ALU.mult))
        link(V.tensor_tensor(t1, t0, t0, ALU.subtract))
        link(V.tensor_scalar(lbs, t1, -1.0, 1.0, ALU.mult, ALU.add))
        link(V.tensor_scalar(par[:, :, 26:28], par[:, :, 26:28], 0.5, None, ALU.mult))
        dve.wait_ge(dt_a, 1)
        link(V.tensor_scalar(hdt[:, :, :].rearrange("p t h -> p (t h)"), v, 0.5, None, ALU.mult))
        link(V.tensor_tensor(v, v, aa, ALU.mult))
        link(V.tensor_scalar(ad[:, :, :].rearrange("p t h -> p (t h)"), v, -1.0, None, ALU.mult))
        for n in range(N_X + 2, N_P0 + 2):
            lo(n, n)
        dve.wait_ge(unit_used, 2 * NH)
        link(V.memset(up[:, :, 0:3], 0.0))
        V.memset(small[:, :, :], 0.0).then_inc(upz, 1)
        dve.wait_ge(upz, 1)
        for n in range(N_P0 + 2, N_P0 + 5):
            lo(n, n)
        with dve.Fori(0, PARTS) as p:
            c = [0]

            def step(ins):
                c[0] += 1
                ins.then_inc(s["vch"], 1)
                dve.wait_ge(s["vch"], cnt(p, VC, c[0]))

            def b3(b):
                return bank[b][:, :].rearrange("p (t c) -> p t c", t=2)

            def par_of(j):
                return prm[:, j:j + 1]

            def conv(i):
                step(V.tensor_scalar(cv[:, i, :], up[:, i, 3:3 + S], par_of(4 * i + 3), par_of(16 + i), ALU.mult, ALU.add))
                for j in range(2, -1, -1):
                    ins = V.scalar_tensor_tensor(cv[:, i, :], up[:, i, j:j + S], par_of(4 * i + j), cv[:, i, :],
                                                 ALU.mult, ALU.add)
                    if j > 0 or i % 2 == 0:
                        step(ins)
                    else:
                        ins.then_inc(s["cv_ok"], 1)
                        dve.wait_ge(s["cv_ok"], cnt(p, 2, 1 + i // 2) + START)

            def lev_step(ins, k):
                ins.then_inc(s["lev_ok"], 1)
                dve.wait_ge(s["lev_ok"], cnt(p, 17, k))

            def level_out(l):
                if l == 0:
                    dve.wait_ge(s["o_ps"], p + START)
                dve.wait_ge(s["lev_ps"], cnt(p, LEVELS - 1, l + 1))
                scores = bank[6][:, :].rearrange("p (b t) -> p b t", t=P)
                if l == 0:
                    lev_step(V.tensor_tensor(att[:, :, :], scores, ident[:, :].unsqueeze(1).broadcast_to([P, 2 * TT, P]),
                                             ALU.mult), 2)
                    lev_step(V.tensor_tensor(flat(qq), flat(qq), fgate[:, :], ALU.mult), 3)
                    return
                m = 2 ** (l - 1)
                nb = 2 * S // (2 * m)
                t = blk[l - 1][:, :].rearrange("p (b o) -> p b o", o=2)
                kv = flat(kk).rearrange("p (b m) -> p b m", m=2 * m)
                qv = flat(qq).rearrange("p (b m) -> p b m", m=2 * m)
                V.tensor_tensor(kv[:, :, 0:m], kv[:, :, 0:m], t[:, :, 1:2].broadcast_to([P, nb, m]), ALU.mult)\
                    .then_inc(s["lev_k"], 1)
                V.copy_predicated(att[:, :, :], lmask[:, l - 1:l, :].broadcast_to([P, 2 * TT, P]), scores)\
                    .then_inc(s["lev_ok"], 1)
                V.tensor_tensor(qv[:, :, m:2 * m], qv[:, :, m:2 * m], t[:, :, 0:1].broadcast_to([P, nb, m]), ALU.mult)\
                    .then_inc(s["lev_ok"], 1)
                if l < LEVELS - 2:
                    step(V.tensor_tensor(blk[l][:, :].rearrange("p (b o) -> p b o", o=1), t[:, :, 0:1], t[:, :, 1:2],
                                         ALU.mult))
                dve.wait_ge(s["lev_ok"], cnt(p, 17, 2 * l + 3))

            def flat(t):
                return t[:, :, :].rearrange("p a b -> p (a b)")

            for u in range(4, UP + 5):
                if u > 4:
                    lo(N_P0 + u, p * UP + (N_P0 + u))
                if u == 4:
                    dve.wait_ge(s["ys_ok"], 2 * p + START)
                    step(V.tensor_copy(prm[:, :], par[:, p, :]))
                    dve.wait_ge(s["dec_ps"], 3 * p + START)
                    for b, t, msk in ((0, 0, True), (2, 0, False), (1, 1, True)):
                        a_b = ad[:, t:t + 1, bass.ts(p, 4)].rearrange("p o h -> p h o").broadcast_to([P, 4, P])
                        if msk:
                            ins = V.tensor_tensor(ta[:, b, :, :], a_b, upto[:, :].unsqueeze(1).broadcast_to([P, 4, P]),
                                                  ALU.mult)
                        else:
                            ins = V.tensor_copy(ta[:, b, :, :], a_b)
                        ins.then_inc(s["ta_ok"], 1)
                if u == 6:
                    dve.wait_ge(s["sc_ps"], p + 1 + START)
                    step(V.tensor_reduce(small[:, 0, 0:2], b3(4), AX.X, ALU.max))
                    dve.wait_ge(s["p_ok"], 2 * p + START)
                    V.tensor_scalar(small[:, 1, 0:2], small[:, 0, 0:2], -(UC ** -0.5), None, ALU.mult)\
                        .then_inc(s["nmx_ok"], 1)
                    dve.wait_ge(s["yp_ps"], p + 1 + START)
                    for j in range(2):
                        V.tensor_scalar(yT[:, 0, p * 2 + j, :], bank[3][:, j * S:(j + 1) * S], par_of(20 + j), None,
                                        ALU.mult).then_inc(s["yp_ok"], 1)
                if u == 7:
                    dve.wait_ge(s["f_exp"], p + 1)
                    step(V.tensor_scalar(fr[:, :, :], fr[:, :, :], 1.0, None, ALU.add))
                    step(V.reciprocal(fr[:, :, :], fr[:, :, :]))
                    for h in range(2):
                        step(V.tensor_scalar(fr[:, h, :], fr[:, h, :], par_of(24 + h), None, ALU.mult))
                    step(V.tensor_scalar(fgate[:, :], flat(fr), -1.0, 1.0, ALU.mult, ALU.add))
                    dve.wait_ge(s["x_ps"], p + START)
                    V.tensor_scalar(flat(kk), flat(fr), 0.5, None, ALU.mult).then_inc(s["kk_ok"], 1)
                    dve.wait_ge(s["kk_ok"], p + 1 + START)
                if u == 8:
                    dve.wait_ge(s["p_ok"], 2 * p + 2 + START)
                    step(V.reciprocal(small[:, 3, 0:2], small[:, 2, 0:2]))
                    step(V.tensor_scalar(prob[:, 0, :], prob[:, 0, :], small[:, 3, 0:1], None, ALU.mult))
                    V.tensor_scalar(prob[:, 1, :], prob[:, 1, :], small[:, 3, 1:2], None, ALU.mult).then_inc(s["pn_ok"], 1)
                    dve.wait_ge(s["qt_ok"], p + 1)
                    lev_step(V.scalar_tensor_tensor(qq[:, :, :], th[:, :, :], 1.0, b3(0), ALU.add, ALU.mult), 1)
                if 9 <= u < 17:
                    level_out(u - 9)
                if u == 11:
                    dve.wait_ge(s["up_ok"], cnt(p, 2, 1))
                    conv(0)
                if u == 12:
                    conv(1)
                if u == 13:
                    dve.wait_ge(s["up_ok"], cnt(p, 2, 2))
                    conv(2)
                    dve.wait_ge(s["tc_ok"], cnt(p, 2, 1))
                    V.scalar_tensor_tensor(cv[:, 0:2, :], tc[:, 0:2, :], 1.0, cv[:, 0:2, :], ALU.add, ALU.mult)\
                        .then_inc(s["xc_ok"], 1)
                if u == 14:
                    conv(3)
                if u == 15:
                    dve.wait_ge(s["tc_ok"], cnt(p, 2, 2))
                    V.scalar_tensor_tensor(cv[:, 2:4, :], tc[:, 2:4, :], 1.0, cv[:, 2:4, :], ALU.add, ALU.mult)\
                        .then_inc(s["xc_ok"], 1)
                    dve.wait_ge(s["gt_ok"], p + 1)
                    V.scalar_tensor_tensor(gs[:, :, :], th[:, :, :], 1.0, b3(0), ALU.add, ALU.mult).then_inc(s["gs_ok"], 1)
                if u == 16:
                    dve.wait_ge(s["xtp_ps"], p + 1)
                    for t in range(TT):
                        V.tensor_tensor(xt[:, t, :].rearrange("p (h c) -> p h c", h=4),
                                        bank[4][:, t * UC:(t + 1) * UC].rearrange("p (h c) -> p h c", h=4),
                                        hdt[:, t:t + 1, bass.ts(p, 4)].rearrange("p o h -> p h o").broadcast_to([P, 4, 64]),
                                        ALU.mult).then_inc(s["xt_ok"], 1)
                if u == 17:
                    dve.wait_ge(s["cb_ps"], p + 1)
                    V.tensor_tensor(cbm[:, :, :], bank[3][:, 0:3 * P].rearrange("p (b l) -> p b l", b=3), quart[:, :, :],
                                    ALU.mult).then_inc(s["cb_ok"], 1)
                    dve.wait_ge(s["cb_ok"], p + 1)
                    dve.wait_ge(s["dec_ok"], 3 * p + 3)
                    V.tensor_tensor(dec[:, :, :, :], dec[:, :, :, :],
                                    cbm[:, :, :].unsqueeze(2).broadcast_to([P, 3, 4, P]), ALU.mult).then_inc(s["g_ok"], 1)
                if u == 19:
                    dve.wait_ge(s["y_ps"], p + 1 + START)
                    for j in range(2):
                        step(V.scalar_tensor_tensor(yss[:, j, :], cv[:, j, :], par_of(26 + j), bank[5][:, j * S:(j + 1) * S],
                                                    ALU.mult, ALU.add))
                    dve.wait_ge(s["tz_ok"], p + 1)
                    step(V.scalar_tensor_tensor(zs[:, :, :], zs[:, :, :], 1.0, b3(2), ALU.add, ALU.mult))
                    V.scalar_tensor_tensor(yss[:, :, :], yss[:, :, :], 0.5, zs[:, :, :], ALU.mult, ALU.mult)\
                        .then_inc(s["y1_ok"], 1)
                if u == 20:
                    dve.wait_ge(s["oss_ps"], p + 1 + START)
                    V.tensor_scalar(rh, bank[3][:, :], 1.0 / P, EPS, ALU.mult, ALU.add).then_inc(s["ovar_ok"], 1)
                    dve.wait_ge(s["yss_ps"], p + 1 + START)
                    V.tensor_scalar(rs[:, :], bank[4][:, 0:S], 1.0 / UC, EPS, ALU.mult, ALU.add).then_inc(s["yvar_ok"], 1)
                if u == 21:
                    dve.wait_ge(s["osd_ok"], p + 1)
                    step(V.reciprocal(rh, rh))
                    step(V.scalar_tensor_tensor(rh, bank[7][:, :], hnw[:, 0:1], rh, ALU.mult, ALU.mult))
                    V.scalar_tensor_tensor(yT[:, 2, bass.ts(p, 2), :], rh.rearrange("p (a b) -> p a b", a=2), 0.5,
                                           gs[:, :, :], ALU.mult, ALU.mult).then_inc(s["yh_ok"], 1)
                if u == 22:
                    dve.wait_ge(s["ysd_ok"], p + 1)
                    step(V.reciprocal(rs[:, :], rs[:, :]))
                    for j in range(2):
                        V.scalar_tensor_tensor(yT[:, 1, p * 2 + j, :], yss[:, j, :], par_of(22 + j), rs[:, :],
                                               ALU.mult, ALU.mult).then_inc(s["ys_ok"], 1)
            assert c[0] == VC, c[0]


        dve.wait_ge(s["ys_ok"], 2 * PARTS + START)
        dve.wait_ge(s["cx_ok"], PARTS)
        dve.wait_ge(s["yss_ps"], PARTS + START)
        dve.wait_ge(mg["y1_hi"], 1)
        V.tensor_tensor(ylo[1][:, :, :], yT[:, 1, :, :], yhi[1][:, :, :].bitcast(f32), ALU.subtract).then_inc(mg["y1_lo"], 1)
        dve.wait_ge(mg["y1_lo"], 1)
        with dve.Fori(0, DBLK) as b:
            c = [0]

            def mstep(ins):
                c[0] += 1
                ins.then_inc(mg["ch"], 1)
                dve.wait_ge(mg["ch"], b * 4 + c[0])

            for u in range(4, UM + 5):
                if u > 4:
                    lo(N_M0 + u, b * UM + (N_M0 + u))
                if u in (4, 6, 9, 12):
                    n = (4, 6, 9, 12).index(u)
                    dve.wait_ge(mg["gate_ok"], b * 4 + (n + 1) + START)
                    dve.wait_ge(unit_used, b * UM + (N_M0 + 3 * n + 3 - N_X))
                    if n == 0:
                        dve.wait_ge(mg["block_ok"], b + START)
                    dst = macc if n == 0 else mtmp
                    V.scalar_tensor_tensor(dst[:, :], sig[:, n, :], 1.0, bank[2 * n + 1][:, :], ALU.add, ALU.mult)\
                        .then_inc(mg["mul_ok"], 1)
                    dve.wait_ge(mg["mul_ok"], b * 4 + (n + 1) + START)
                    if n > 0:
                        mstep(V.tensor_tensor(macc[:, :], macc[:, :], mtmp[:, :], ALU.add))
                if u == UM:
                    dve.wait_ge(mg["y_lo"], 3)
                    acc3 = macc[:, :].rearrange("p (c t) -> p c t", c=2)
                    gh, gl = ghi[:, bass.ts(b, 2), :], glo[:, bass.ts(b, 2), :]
                    mstep(V.tensor_scalar(gh, acc3, 0.5, None, ALU.mult))
                    V.scalar_tensor_tensor(gl, acc3, 0.5, gh.bitcast(f32), ALU.mult, ALU.subtract)\
                        .then_inc(mg["block_ok"], 1)
            assert c[0] == 4

        def residual(cnt_used, cols, k):
            dve.wait_ge(unit_used, cnt_used)
            hs = htok[:, :, cols]
            V.scalar_tensor_tensor(hs, hs, ALPHA, bank[k % 3][:, :].rearrange("p (t c) -> p t c", t=TT), ALU.mult,
                                   ALU.add).then_inc(og["res_ok"], 1)

        dve.wait_ge(og["x_in"], 16 * TT)
        residual(N_O0 + 2 - N_X, slice(0, UC), 0)
        for u in range(5, 16):
            lo(N_O0 + u, N_O0 + u)
            if u % 2 == 1:
                k = (u - 3) // 2
                if k < 6:
                    residual(N_O0 + 2 * k + 2 - N_X, slice(k * UC, (k + 1) * UC), k)

        lch = [0]

        def lstep(ins):
            lch[0] += 1
            ins.then_inc(rt["ch"], 1)
            dve.wait_ge(rt["ch"], lch[0])

        def chunk_stats(src, c):
            for t in range(TT):
                lstep(V.bn_stats(bns[:, t, c, :], src[:, t, c * 512:(c + 1) * 512]))

        def norm_stats(k):
            for t in range(TT):
                lstep(V.bn_aggr(bna[:, t, :], bns[:, t, :, :]))
            V.tensor_scalar(bnr[:, :, 0:1], bna[:, :, 1:2], EPS, None, ALU.add).then_inc(og["stats_ok"], 1)
            dve.wait_ge(og["sd_ok"], k + 1)
            lstep(V.reciprocal(bnr[:, :, 2:3], bnr[:, :, 1:2]))

        def norm_scale(k, t, sl):
            v = (htok, acc)[k][:, t, sl]
            lstep(V.scalar_tensor_tensor(v, v, bna[:, t, 0:1], lng[k][:, sl], ALU.subtract, ALU.mult))
            V.scalar_tensor_tensor(v, v, bnr[:, t, 2:3], lnb[k][:, sl], ALU.mult, ALU.add).then_inc(og["scaled_ok"], 1)

        dve.wait_ge(og["res_ok"], 6 + START)
        for c in range(3):
            chunk_stats(htok, c)
        dve.wait_ge(og["whi_ok"], 1)
        V.tensor_tensor(wrt_st[:, :, E:2 * E], wrt_raw[:, :, :], wrt_st[:, :, 0:E].bitcast(f32), ALU.subtract)\
            .then_inc(og["wlo_ok"], 1)
        lstep(V.tensor_tensor(stack_id[:, :], ident[:, 0:E], ident[:, E:2 * E], ALU.add))
        for k in range(6, 8):
            residual(N_O0 + 2 * k + 2 - N_X, slice(k * UC, (k + 1) * UC), k)
        dve.wait_ge(og["res_ok"], DBLK + START)
        chunk_stats(htok, 3)
        norm_stats(0)
        dve.wait_ge(og["ln_in"], 32)

        def h_low(k2):
            dve.wait_ge(og["hi_ok"], k2 + 1)
            sl = slice(2 * k2, 2 * k2 + 2)
            V.tensor_tensor(hlo[:, sl, :], bank[3 + k2 % 4][:, :].rearrange("p (k t) -> p k t", k=2),
                            hhi[:, sl, :].bitcast(f32), ALU.subtract).then_inc(og["lo_ok"], 1)

        for c in range(4):
            for t in range(TT):
                norm_scale(0, t, slice(c * 512, (c + 1) * 512))
            if c > 0:
                h_low(2 * c - 2)
                h_low(2 * c - 1)
        h_low(6)
        h_low(7)
        for n in (N_S0, N_S0 + 1):
            lo(n, n)
        for n in (N_S0 + 2, N_S0 + 3):
            lo(n, n)
        dve.wait_ge(og["w_in"], 32)
        dve.wait_ge(rt["exp_ok"], 1)
        lstep(V.tensor_scalar(score[:, :, :], score[:, :, :], 1.0, None, ALU.add))
        lstep(V.reciprocal(score[:, :, :], score[:, :, :]))
        lstep(V.tensor_tensor(choice[:, :, :], score[:, :, :], rbias_t[:, :].unsqueeze(1).broadcast_to(EE), ALU.add))
        for t in range(TT):
            for g in range(GROUPS):
                lstep(V.max(gmax[:, t, g, :], choice[:, t, g * 8:(g + 1) * 8]))
        lo(N_D0, N_D0)
        dve.wait_ge(sh["th_ok"], 1)
        lstep(V.scalar_tensor_tensor(sact[:, :], sth[:, :], 1.0, bank[0][:, :], ALU.add, ALU.mult))
        dve.wait_ge(unit_used, N_D0 - N_X)
        V.scalar_tensor_tensor(sact[:, :], sact[:, :], 0.5, bank[1][:, :], ALU.mult, ALU.mult).then_inc(sh["a_ok"], 1)
        dve.wait_ge(sh["hi_ok"], 1)
        V.tensor_tensor(slo[:, :, :], sact[:, :].rearrange("p (c t) -> p c t", c=2), shi[:, :, :].bitcast(f32),
                        ALU.subtract).then_inc(sh["lo_ok"], 1)
        lo(N_D0 + 1, N_D0 + 1)
        lstep(V.tensor_tensor(gsum[:, :, :], gmax[:, :, :, 0], gmax[:, :, :, 1], ALU.add))
        ga = gsum[:, :, :].unsqueeze(2).broadcast_to([P, TT, GROUPS, GROUPS])
        gb = gsum[:, :, :].unsqueeze(3).broadcast_to([P, TT, GROUPS, GROUPS])
        lstep(V.tensor_tensor(gcmp[:, :, :, :], ga, gb, ALU.is_equal))
        lstep(V.tensor_tensor(gcmp[:, :, :, :], gcmp[:, :, :, :],
                              glt[:, :, :].unsqueeze(1).broadcast_to([P, TT, GROUPS, GROUPS]), ALU.mult))
        lstep(V.tensor_tensor(gcmp2[:, :, :, :], ga, gb, ALU.is_gt))
        lstep(V.tensor_tensor(gcmp[:, :, :, :], gcmp[:, :, :, :], gcmp2[:, :, :, :], ALU.add))
        lstep(V.tensor_reduce(gpen[:, :, :], gcmp[:, :, :, :], AX.X, ALU.add))
        lstep(V.tensor_scalar(gmask[:, :, :], gpen[:, :, :], float(TOPG), None, ALU.is_lt))
        lstep(V.tensor_scalar(gpen[:, :, :], gmask[:, :, :], 1.0, -MASK_SCORE, ALU.subtract, ALU.mult))
        shape8 = [P, TT, GROUPS, E // GROUPS]
        v8 = lambda a: a[:, :, :].rearrange("p t (g e) -> p t g e", g=GROUPS)
        lstep(V.tensor_tensor(v8(masked), v8(choice), gmask[:, :, :].unsqueeze(3).broadcast_to(shape8), ALU.mult))
        lstep(V.tensor_tensor(v8(masked), v8(masked), gpen[:, :, :].unsqueeze(3).broadcast_to(shape8), ALU.add))
        for t in range(TT):
            lstep(V.max(top8[:, t, :], masked[:, t, :]))
            lstep(V.match_replace(repl[:, t, :], top8[:, t, :], masked[:, t, :], -3e38))
        V.tensor_tensor(sel[:, :, :], masked[:, :, :], repl[:, :, :], ALU.not_equal).then_inc(rt["sel_ok"], 1)
        def acc_start(chunks):
            for i in chunks:
                j, t, cc = i // 4, i // 2 % 2, i % 2
                dve.wait_ge(sh["dps"], i + 1)
                sl = slice(j * 1024 + cc * 512, j * 1024 + (cc + 1) * 512)
                V.scalar_tensor_tensor(acc[:, t, sl], htok[:, t, sl], ALPHA, bank[2 + i % 5][:, :], ALU.mult, ALU.add)\
                    .then_inc(sh["acc_ok"], 1)

        dve.wait_ge(rt["ps"], 1)
        acc_start(range(4))
        dve.wait_ge(rt["sel_ok"], 1)
        lstep(V.tensor_tensor(wsel[:, :, :], score[:, :, :], sel[:, :, :], ALU.mult))
        lstep(V.tensor_reduce(wsum[:, :, 0:1], wsel[:, :, :], AX.X, ALU.add))
        lstep(V.reciprocal(wsum[:, :, 1:2], wsum[:, :, 0:1]))
        lstep(V.memset(rank[:, :, :], -1000.0))
        lstep(V.memset(wgt[:, :, :], 0.0))
        for t in range(TT):
            lstep(V.tensor_scalar(wgt[:, t, 0:E], wsel[:, t, :], wsum[:, t, 1:2], ROUTED_SCALE, ALU.mult, ALU.mult))
        dve.wait_ge(rt["rk_ps"], 1)
        lstep(V.tensor_scalar(rtmp[:, :, :], bank[7][:, 0:2 * E].rearrange("p (t e) -> p t e", t=TT), 1000.0, None, ALU.add))
        lstep(V.tensor_tensor(rtmp[:, :, :], rtmp[:, :, :], sel[:, :, :], ALU.mult))
        lstep(V.tensor_scalar(rank[:, :, 0:E], rtmp[:, :, :], 1000.0, None, ALU.subtract))
        lstep(V.tensor_reduce(rcnt[:, 0:1], bank[7][:, 2 * E:3 * E], AX.X, ALU.max))
        lstep(V.tensor_scalar(rcnt[:, 1:2], rcnt[:, 0:1], float(CAP), None, ALU.is_gt))
        lstep(V.tensor_scalar(rcnt[:, 2:3], rcnt[:, 0:1], float(2 * CAP), rcnt[:, 1:2], ALU.is_gt, ALU.add))
        lstep(V.tensor_scalar(rcnt[:, 3:4], rcnt[:, 0:1], float(3 * CAP), rcnt[:, 2:3], ALU.is_gt, ALU.add))
        V.tensor_scalar(rounds[:, 0:1], rcnt[:, 3:4], 1.0, None, ALU.add).then_inc(rt["rounds_ok"], 1)
        acc_start(range(4, 8))
        dve.wait_ge(sh["acc_ok"], 8)
        dve.wait_ge(rt["rounds_ok"], 1)
        dve.wait_ge(unit_used, N_UNITS - N_X)
        n_rounds = dve.value_load(rounds[0:1, 0:1], min_val=1, max_val=4)
        with dve.Fori(0, n_rounds) as b:
            PK = PAIRS + 2

            def choose(g):
                r = rank[:, :, bass.ds(g * 2, 2)].unsqueeze(3).broadcast_to([P, TT, 2, CAP])
                sl = slots[:, :].unsqueeze(1).unsqueeze(1).broadcast_to([P, TT, 2, CAP])
                V.tensor_tensor(pick[:, :, :, :], sl, r, ALU.is_equal).then_inc(ex["pick_ok"], 1)

            def gathered(g, used):
                dve.wait_ge(ex["gu_free"], used * 4 + START)
                for k4 in (1, 3):
                    dve.wait_ge(ex["ga_ps"], b * (4 * PAIRS + 4) + (g * 4 + k4 + 1) + START)
                    V.tensor_copy(xg[:, 4 * k4:4 * k4 + 4, :], bank[1][:, :].rearrange("p (k s) -> p k s", k=4))\
                        .then_inc(ex["xg_dve"], 1)

            def add_out(i):
                for t in range(TT):
                    for c in range(4):
                        dve.wait_ge(ex["sc_ps"], b * (8 * PAIRS + 8) + (i * 8 + 4 * t + c + 1))
                        a = acc[:, t, c * 512:(c + 1) * 512]
                        V.tensor_tensor(a, a, bank[6 + c % 2][:, :], ALU.add).then_inc(ex["acc_ok"], 1)

            dve.wait_ge(ex["ga_ps"], b * (4 * PAIRS + 4) + START)
            choose(0)
            gathered(0, b * PAIRS)
            choose(1)
            V.memset(yehi[:, :].bitcast(f32), 0.0).then_inc(ex["zero"], 1)
            V.memset(yelo[:, :].bitcast(f32), 0.0).then_inc(ex["zero"], 1)
            V.memset(pickT[:, :, :].bitcast(f32), 0.0).then_inc(ex["zero"], 1)
            with dve.Fori(0, PAIRS) as pair:
                it = b * PAIRS + pair
                dve.wait_ge(ex["th_ok"], it + 1)
                dve.wait_ge(ex["at_ps"], it + START)
                V.scalar_tensor_tensor(eact[:, :], eth[:, :], 1.0, bank[3][:, 0:FE], ALU.add, ALU.mult).then_inc(ex["ch"], 1)
                dve.wait_ge(ex["ch"], it + 1)
                V.scalar_tensor_tensor(eact[:, :], eact[:, :], 0.5, bank[3][:, FE:2 * FE], ALU.mult, ALU.mult)\
                    .then_inc(ex["a_ok"], 1)
                dve.wait_ge(ex["pt_ps"], it + START)
                r = rank[:, :, bass.ds(pair * 2, 2)].unsqueeze(3).broadcast_to([P, TT, 2, CAP])
                sl = slots[:, :].unsqueeze(1).unsqueeze(1).broadcast_to([P, TT, 2, CAP])
                V.tensor_tensor(pickw[:, :, :, :], sl, r, ALU.is_equal).then_inc(ex["round_end"], 1)
                dve.wait_ge(ex["round_end"], b * (PAIRS + 1) + (pair + 1))
                V.tensor_tensor(pickw[:, :, :, :], pickw[:, :, :, :],
                                wgt[:, :, bass.ds(pair * 2, 2)].unsqueeze(3).broadcast_to([P, TT, 2, CAP]), ALU.mult)\
                    .then_inc(ex["pickw_ok"], 1)
                gathered(pair + 1, it + 1)
                choose(pair + 2)
                dve.wait_ge(ex["acc_ok"], b * (8 * PAIRS + 8) + pair * 8 + START)
                add_out(pair)
                dve.wait_ge(ex["wslot_ok"], it + 1)
                V.tensor_scalar(pickT[:, :, :], bank[2][:, S:2 * S].rearrange("p (t s) -> p t s", t=TT), 0.0, None,
                                ALU.is_gt).then_inc(ex["pt_ok"], 1)
                for c in range(4):
                    dve.wait_ge(ex["y_ok"], it * 4 + (c + 1) + START)
                    sl = slice(c * 512, (c + 1) * 512)
                    V.scalar_tensor_tensor(yelo[:, sl], bank[4 + c % 2][:, :], wslot[:, :], yehi[:, sl].bitcast(f32),
                                           ALU.mult, ALU.subtract).then_inc(ex["y_split"], 1)
            dve.wait_ge(ex["acc_ok"], b * (8 * PAIRS + 8) + 8 * PAIRS + START)
            add_out(PAIRS)
            dve.wait_ge(ex["pick_ok"], b * PK + PK)
            dve.wait_ge(ex["pickw_ok"], b * PAIRS + PAIRS)
            dve.wait_ge(ex["sc_ps"], b * (8 * PAIRS + 8) + (8 * PAIRS + 8))
            V.tensor_scalar(rank[:, :, :], rank[:, :, :], float(CAP), None, ALU.subtract).then_inc(ex["round_end"], 1)
            dve.wait_ge(ex["round_end"], b * (PAIRS + 1) + (PAIRS + 1))
            dve.wait_ge(ex["acc_ok"], b * (8 * PAIRS + 8) + (8 * PAIRS + 8) + START)
        dve.wait_ge(ex["g2"], 32)
        for c in range(4):
            chunk_stats(acc, c)
        norm_stats(1)
        for t in range(TT):
            for c in range(4):
                norm_scale(1, t, slice(c * 512, (c + 1) * 512))

    blkctx.__exit__(None, None, None)


def _unit(w):
    return w.reshape(UK, P, UC).transpose(1, 0, 2).reshape(P, UK * UC)


def _columns(w):
    return [_unit(w[k:k + UK * P]) for k in range(0, w.shape[0], UK * P)]


def kernel(**inputs):
    import numpy as np
    import concourse.bacc as bacc
    from concourse.bass_utils import run_bass_kernel_spmd

    v = {k: np.asarray(a) for k, a in inputs.items()}
    w_in, w_branch = v["w_in"][0], v["w_branch"][0]
    W = PARTS * UC
    o_pool, o_z, o_xbc = 0, W, 2 * W
    o_dt = 4 * W
    o_q, o_f, o_i, o_g, o_mem, o_gate = (o_dt + 16 + W * j for j in range(6))
    units = _columns(v["x"][0].T) + _columns(v["mem"][0].T)
    for c in range(2 * PARTS):
        units += _columns(v["w_mem_kv"][0][:, c * UC:(c + 1) * UC])
    for p in range(PARTS):
        for o in (o_mem, o_pool, o_f, o_q, o_xbc):
            units += _columns(w_in[:, o + p * UC:o + (p + 1) * UC])
        o_b, o_c = o_xbc + W + p * P, o_xbc + W + W // 2 + p * P
        units += _columns(np.concatenate([w_in[:, o_b:o_b + P], w_in[:, o_c:o_c + P]], axis=1))
        for o in (o_g, o_i, o_z):
            units += _columns(w_in[:, o + p * UC:o + (p + 1) * UC])
    for b in range(DBLK):
        for n in range(4):
            units += _columns(w_in[:, o_gate + n * D + b * UC:o_gate + n * D + (b + 1) * UC])
            units += _columns(w_branch[n][:, b * UC:(b + 1) * UC])
    for b in range(DBLK):
        units += _columns(v["w_o"][0][:, b * UC:(b + 1) * UC])
    units += _columns(v["w_sh_gate"][0]) + _columns(v["w_sh_up"][0])
    for c in range(2):
        w = v["w_sh_down"][0][:, c * 1024:(c + 1) * 1024]
        units.append(w.reshape(2, P, 1024).transpose(1, 0, 2).reshape(P, UK * UC))

    params = np.zeros((P, PARTS, NP), np.float32)
    for p in range(PARTS):
        for t, c in enumerate((p * UC, p * UC + P, W + p * P, W + W // 2 + p * P)):
            params[:, p, 4 * t:4 * t + 4] = v["conv_w"][0][:, c:c + P].T
            params[:, p, 16 + t] = v["conv_b"][0][c:c + P]
        for j in range(2):
            c = p * UC + j * P
            params[:, p, 20 + j] = v["pool_scale"][0][c:c + P]
            params[:, p, 22 + j] = v["ssd_norm"][0][c:c + P]
            params[:, p, 24 + j] = v["hgrn_lb"][0][c:c + P]
            params[:, p, 26 + j] = np.repeat(v["d_skip"][0][4 * p + 2 * j:4 * p + 2 * j + 2], 64)
    pool = np.zeros((PARTS, S, S), np.float32)
    for g in range(PARTS):
        for t in range(S):
            first = max(t + 1 - 2 ** (g + 1), 0)
            pool[g, first:t + 1, t] = 1.0 / (t + 1 - first)
            pool[g, t, t] -= 1.0

    def tiles(w):
        return w.reshape(-1, P, w.shape[-1]).transpose(1, 0, 2)

    gate_up = np.concatenate([v["w_exp_gate"][0], v["w_exp_up"][0]], axis=2)
    arrays = {
        "units": np.stack(units),
        "params": params,
        "hnorm": v["hgrn_norm"][0][:, None],
        "wdt": tiles(w_in[:, o_dt:o_dt + 16]).reshape(P, KT * 16),
        "dtb": np.broadcast_to(np.tile(v["dt_bias"][0], TT), (P, TT * 16)),
        "alog": np.broadcast_to(np.tile(v["a_log"][0], TT), (P, TT * 16)),
        "poolm": pool.reshape(PARTS, TT, P, S).transpose(0, 2, 1, 3),
        "poolw": v["pool_w"][0].reshape(PARTS, 2, P, UC).transpose(0, 2, 1, 3),
        "xtok": v["x"][0],
        "lnp": np.stack([v["ln1_g"][0], v["ln1_b"][0], v["ln2_g"][0], v["ln2_b"][0]]),
        "wrt": tiles(v["w_router"][0]),
        "rbias": v["router_bias"][0],
        "wgu": gate_up.reshape(E, 4, 4, P, 2 * FE).transpose(0, 1, 3, 2, 4),
        "wd": v["w_exp_down"][0].reshape(E, 2, P, D),
    }
    arrays = {k: np.ascontiguousarray(a) for k, a in arrays.items()}
    nc = bacc.Bacc("TRN2", target_bir_lowering=False, num_devices=1)
    handles = [nc.dram_tensor(k, a.shape, mybir.dt.from_np(a.dtype), kind="ExternalInput").ap() for k, a in arrays.items()]
    out = nc.dram_tensor("out", (S, D), f32, kind="ExternalOutput").ap()
    build_trunk(nc, *handles, out)
    r = run_bass_kernel_spmd(nc, [arrays], core_ids=[0])
    return r.results[0]["out"].reshape(1, S, D)
```
